# Optimizing a Trainium2 kernel written in Bass

```python
import math
import jax, jax.numpy as jnp
from jax import lax
import numpy as np

D_MODEL = 1024
BATCH = 1
SEQ = 512
DEPTH = 1

HEAD_DIM = 64
D_MIX = D_MODEL
D_MOBA = D_MIX // 2
D_RET = D_MIX - D_MOBA
N_HEADS_MOBA = D_MOBA // HEAD_DIM
N_HEADS_RET = D_RET // HEAD_DIM
N_PROJ = 3 * D_MOBA + 4 * D_RET
MOBA_BLOCK = 256
MOBA_TOPK = 3
Q_BLOCK = 128
RET_CHUNK = 256
REL_BUCKETS = 32
REL_MAX_DIST = 128
ROPE_BASE = 10000.0
D_FF = ((8 * D_MODEL // 3 + 255) // 256) * 256
CONV_WIDTH = 3
EPS = 1e-6
NEG = -1e30

kernel_name = 'hybrid_moba_retention_block'

def rmsnorm(x, g):
    xf = x.astype(jnp.float32)
    y = xf * lax.rsqrt(jnp.mean(xf * xf, axis=-1, keepdims=True) + EPS)
    return (y * g.astype(jnp.float32)).astype(x.dtype)

def t5_bucket(rel):
    n = jnp.maximum(rel, 0)
    max_exact = REL_BUCKETS // 2
    n_f = jnp.maximum(n, 1).astype(jnp.float32)
    large = max_exact + (jnp.log(n_f / max_exact) / math.log(REL_MAX_DIST / max_exact)
                         * (REL_BUCKETS - max_exact)).astype(jnp.int32)
    large = jnp.minimum(large, REL_BUCKETS - 1)
    return jnp.where(n < max_exact, n, large)

def moba_attention(q, k, v, rel_bias):
    B, H, S, D = q.shape
    nb = S // MOBA_BLOCK
    n_sel = min(MOBA_TOPK, nb)
    scale = D ** -0.5
    kb = k.reshape(B, H, nb, MOBA_BLOCK, D)
    vb = v.reshape(B, H, nb, MOBA_BLOCK, D)
    k_mean = jnp.mean(kb.astype(jnp.float32), axis=3).astype(k.dtype)
    bias_t = rel_bias.T.astype(jnp.float32)
    head_ix = jnp.arange(H)[None, :, None, None, None]
    blk_pos = jnp.arange(MOBA_BLOCK, dtype=jnp.int32)
    gather = jax.vmap(jax.vmap(lambda blocks, ix: blocks[ix]))

    def one_query_block(i):
        q0 = i * Q_BLOCK
        qi = lax.dynamic_slice_in_dim(q, q0, Q_BLOCK, axis=2)
        t = q0 + jnp.arange(Q_BLOCK, dtype=jnp.int32)
        c = q0 // MOBA_BLOCK
        gate = jnp.einsum('bhqd,bhnd->bhqn', qi, k_mean).astype(jnp.float32)
        gate = jnp.where(jnp.arange(nb) < c, gate, -jnp.inf)
        _, idx = lax.top_k(gate, n_sel)
        valid = idx < c
        k_sel = gather(kb, idx)
        v_sel = gather(vb, idx)
        s_sel = jnp.einsum('bhqd,bhqnkd->bhqnk', qi, k_sel).astype(jnp.float32) * scale
        pos_sel = idx[..., None] * MOBA_BLOCK + blk_pos
        bias_sel = bias_t[head_ix, t5_bucket(t[:, None, None] - pos_sel)]
        s_sel = jnp.where(valid[..., None], s_sel + bias_sel, NEG)
        k_own = lax.dynamic_slice_in_dim(k, c * MOBA_BLOCK, MOBA_BLOCK, axis=2)
        v_own = lax.dynamic_slice_in_dim(v, c * MOBA_BLOCK, MOBA_BLOCK, axis=2)
        rel_own = t[:, None] - (c * MOBA_BLOCK + blk_pos)[None, :]
        s_own = jnp.einsum('bhqd,bhkd->bhqk', qi, k_own).astype(jnp.float32) * scale
        bias_own = bias_t[:, t5_bucket(rel_own)]
        s_own = jnp.where(rel_own >= 0, s_own + bias_own, NEG)
        logits = jnp.concatenate(
            [s_sel.reshape(B, H, Q_BLOCK, n_sel * MOBA_BLOCK), s_own], axis=-1)
        p = jax.nn.softmax(logits, axis=-1).astype(v.dtype)
        p_sel = p[..., :n_sel * MOBA_BLOCK].reshape(B, H, Q_BLOCK, n_sel, MOBA_BLOCK)
        p_own = p[..., n_sel * MOBA_BLOCK:]
        return (jnp.einsum('bhqnk,bhqnkd->bhqd', p_sel, v_sel)
                + jnp.einsum('bhqk,bhkd->bhqd', p_own, v_own))

    outs = lax.map(one_query_block, jnp.arange(S // Q_BLOCK, dtype=jnp.int32))
    return outs.transpose(1, 2, 0, 3, 4).reshape(B, H, S, D)

def rotary(x):
    S, D = x.shape[2], x.shape[3]
    inv = ROPE_BASE ** (-jnp.arange(0, D, 2, dtype=jnp.float32) / D)
    ang = jnp.arange(S, dtype=jnp.float32)[:, None] * inv[None, :]
    cos, sin = jnp.cos(ang), jnp.sin(ang)
    x1, x2 = x[..., :D // 2], x[..., D // 2:]
    return jnp.concatenate([x1 * cos - x2 * sin, x1 * sin + x2 * cos], axis=-1)

def retention(q, k, v, g):
    B, H, S, D = q.shape
    C = RET_CHUNK
    NC = S // C
    qf = rotary(q.astype(jnp.float32))
    kf = rotary(k.astype(jnp.float32)) * (D ** -0.5)
    vf = v.astype(jnp.float32)
    log_gamma = jnp.log(1.0 - 2.0 ** (-5.0 - jnp.arange(H, dtype=jnp.float32)))
    n = jnp.arange(C, dtype=jnp.float32)
    rel = n[:, None] - n[None, :]
    decay_mask = jnp.where(rel >= 0, jnp.exp(jnp.maximum(rel, 0.0)[None] * log_gamma[:, None, None]), 0.0)
    qc = qf.reshape(B, H, NC, C, D)
    kc = kf.reshape(B, H, NC, C, D)
    vc = vf.reshape(B, H, NC, C, D)
    scores = jnp.einsum('bhcnd,bhcmd->bhcnm', qc, kc) * decay_mask[None, :, None]
    y_inner = jnp.einsum('bhcnm,bhcme->bhcne', scores, vc)
    decay_end = jnp.exp((C - 1.0 - n)[None, :] * log_gamma[:, None])
    kv = jnp.einsum('bhcmd,bhcme->bhcde', kc * decay_end[None, :, None, :, None], vc)
    chunk_decay = jnp.exp(C * log_gamma)[None, :, None, None]

    def step(state, kv_c):
        return state * chunk_decay + kv_c, state

    _, r_prev = lax.scan(step, jnp.zeros((B, H, D, D), jnp.float32), jnp.moveaxis(kv, 2, 0))
    r_prev = jnp.moveaxis(r_prev, 0, 2)
    decay_start = jnp.exp((n + 1.0)[None, :] * log_gamma[:, None])
    y_cross = jnp.einsum('bhcnd,bhcde->bhcne', qc, r_prev) * decay_start[None, :, None, :, None]
    y = (y_inner + y_cross).reshape(B, H, S, D)
    mu = jnp.mean(y, axis=-1, keepdims=True)
    var = jnp.mean(jnp.square(y - mu), axis=-1, keepdims=True)
    y = (y - mu) * lax.rsqrt(var + EPS)
    y = y.transpose(0, 2, 1, 3).reshape(B, S, H * D)
    return (jax.nn.silu(g.astype(jnp.float32)) * y).astype(q.dtype)

def setup_inputs(seed: int = 0) -> dict:
    key = jax.random.key(seed)
    ks = jax.random.split(key, 12)
    L = DEPTH

    def nrm(k, shape, scale):
        return jax.random.normal(k, shape, jnp.float32) * scale

    return {
        'x': nrm(ks[0], (BATCH, SEQ, D_MODEL), 1.0),
        'norm_mix_pre': 1.0 + nrm(ks[1], (L, D_MODEL), 0.05),
        'w_in': nrm(ks[2], (L, D_MODEL, N_PROJ), D_MODEL ** -0.5),
        'rel_bias': nrm(ks[3], (REL_BUCKETS, N_HEADS_MOBA), 0.5),
        'w_out': nrm(ks[4], (L, D_MIX, D_MODEL), D_MIX ** -0.5),
        'norm_mix_post': 1.0 + nrm(ks[5], (L, D_MODEL), 0.05),
        'norm_ffn_pre': 1.0 + nrm(ks[6], (L, D_MODEL), 0.05),
        'w_up': nrm(ks[7], (L, D_MODEL, 2 * D_FF), D_MODEL ** -0.5),
        'conv_w': nrm(ks[8], (L, CONV_WIDTH, 2 * D_FF), CONV_WIDTH ** -0.5),
        'conv_b': nrm(ks[9], (L, 2 * D_FF), 0.02),
        'w_down': nrm(ks[10], (L, D_FF, D_MODEL), D_FF ** -0.5),
        'norm_ffn_post': 1.0 + nrm(ks[11], (L, D_MODEL), 0.05),
    }

def reference(x, norm_mix_pre, w_in, rel_bias, w_out, norm_mix_post,
              norm_ffn_pre, w_up, conv_w, conv_b, w_down, norm_ffn_post):
    B, S, _ = x.shape
    S_pad = -(-S // MOBA_BLOCK) * MOBA_BLOCK

    def heads(t, n_heads):
        return t.reshape(B, S_pad, n_heads, HEAD_DIM).transpose(0, 2, 1, 3)

    for l in range(DEPTH):
        h = rmsnorm(x, norm_mix_pre[l])
        proj = jnp.einsum('bsd,dn->bsn', h, w_in[l])
        proj = jnp.pad(proj, ((0, 0), (0, S_pad - S), (0, 0)))
        qa, ka, va, qr, kr, vr, gr = jnp.split(
            proj, np.cumsum([D_MOBA, D_MOBA, D_MOBA, D_RET, D_RET, D_RET])[:].tolist(), axis=-1)
        ya = moba_attention(heads(qa, N_HEADS_MOBA), heads(ka, N_HEADS_MOBA),
                            heads(va, N_HEADS_MOBA), rel_bias)
        ya = ya.transpose(0, 2, 1, 3).reshape(B, S_pad, D_MOBA)
        yr = retention(heads(qr, N_HEADS_RET), heads(kr, N_HEADS_RET),
                       heads(vr, N_HEADS_RET), gr)
        y = jnp.concatenate([ya, yr], axis=-1)[:, :S]
        y = jnp.einsum('bsn,nd->bsd', y, w_out[l])
        x = x + rmsnorm(y, norm_mix_post[l])
        h = rmsnorm(x, norm_ffn_pre[l])
        u = jnp.einsum('bsd,df->bsf', h, w_up[l])
        up = jnp.pad(u, ((0, 0), (CONV_WIDTH - 1, 0), (0, 0)))
        u = conv_b[l] + sum(conv_w[l, j] * up[:, j:j + S] for j in range(CONV_WIDTH))
        a, b = jnp.split(u, 2, axis=-1)
        f = jax.nn.gelu(a, approximate=True) * b
        y = jnp.einsum('bsf,fd->bsd', f, w_down[l])
        x = x + rmsnorm(y, norm_ffn_post[l])
    return x


_drawn_inputs = setup_inputs


def setup_inputs(seed=0):
    import zlib

    import numpy as np

    out = dict(_drawn_inputs(seed))
    spreads = {}
    factors = {'conv_b': 3.396}
    for name, (base, spread) in spreads.items():
        noise = np.random.default_rng([zlib.crc32(name.encode()), seed]).standard_normal(out[name].shape)
        drawn = base * np.exp(spread * noise) if base else spread * noise
        out[name] = __import__('jax').numpy.asarray(drawn.astype(out[name].dtype))
    for name, factor in factors.items():
        out[name] = (out[name] * factor).astype(out[name].dtype)
    return out
```

```python
import math
from contextlib import ExitStack

import concourse.bass as bass
import numpy as np
from concourse import mybir

F32 = mybir.dt.float32
F32R = mybir.dt.float32r
ALU = mybir.AluOpType
ACT = mybir.ActivationFunctionType
AX = mybir.AxisListType

P = 128
SEQ, D = 512, 1024
HD = 64
HEADS = 8
DMIX = HEADS * HD
PAIRS = HEADS // 2
DFF = 2816
FT = DFF // P
KT = D // P
ST = SEQ // P
EPS = 1e-6
BUCKETS, MAX_DIST = 32, 128
VEC = SEQ + P
GROUPS = [1, 0, 2, 4, 3, 5, 6]
KA, QA, VA, KR, QR, VR, GR = range(7)
NU = 7
OUT0 = NU * PAIRS
UP0 = OUT0 + 2 * KT
DOWN0 = UP0 + 2 * FT
SWEEP = FT // 2
LAST_UNIT = DOWN0 + 2 * SWEEP
SLOTS = 4


def slot_of(n):
    if n < OUT0:
        return n % NU % SLOTS
    if n < DOWN0:
        return (n - OUT0) % SLOTS
    k = (n - DOWN0) % SWEEP
    return 2 if k == SWEEP - 1 else k % 2


def loads_of_slot(n):
    return sum(slot_of(m) == slot_of(n) for m in range(n + 1))


def freed_at(n):
    if n >= DOWN0:
        return n - 1
    return max((m + 1 for m in range(n) if slot_of(m) == slot_of(n)), default=0)


def at_turn(f, n, i, per_turn):
    if isinstance(i, int):
        return f(n + i * per_turn)
    a, b = f(n + per_turn), f(n + 2 * per_turn)
    return (b - a) * i + (2 * a - b)


def window(dram, head, rows):
    return bass.AP(dram, head * VEC, [[1, P], [VEC, rows], [1, SEQ]])


def build(nc, x, norm_mix_pre, w_in, rel_bias, w_out, norm_mix_post, norm_ffn_pre, w_up,
          conv_w, conv_b, w_down, norm_ffn_post, rotary, decay, onehot, out):
    ctx = ExitStack()
    with ctx:
        def sb(name, shape, dt=F32):
            return ctx.enter_context(nc.sbuf_tensor(name, shape, dt))

        def sem(name):
            return ctx.enter_context(nc.semaphore(name))

        xs = sb("xs", [P, ST, D])
        hT = sb("hT", [P, 2, KT, SEQ], F32R)
        yT = sb("yT", [P, 2, KT, SEQ], F32R)
        ws = sb("ws", [P, SLOTS, 2, D], F32R)
        raw = sb("raw", [P, SLOTS, D])
        gains = sb("gains", [P, 2, D])
        ident = sb("ident", [P, P])
        rot = sb("rot", [P, 2, SEQ])
        convrows = sb("convrows", [2 * FT, 4, P])
        conv = sb("conv", [P, 4 * 2 * FT])
        relb = sb("relb", [BUCKETS + 1, HEADS])
        oneh = sb("oneh", [BUCKETS + 1, VEC])
        bvec = sb("bvec", [HEADS, VEC])
        neghalf = sb("neghalf", [P, 8])
        sumsq = sb("sumsq", [P, 16])
        meansq = sb("meansq", [P, 16])
        rstd = sb("rstd", [P, 16])
        osum = sb("osum", [P, 2 * ST, 2])
        negmax = sb("negmax", [P, HEADS])
        rowsum = sb("rowsum", [P, HEADS])
        rowinv = sb("rowinv", [P, HEADS])
        gsum = sb("gsum", [P, HEADS])
        gneg = sb("gneg", [P, HEADS])
        gvar = sb("gvar", [P, HEADS])
        gms = sb("gms", [P, HEADS])
        grstd = sb("grstd", [P, HEADS])
        work = sb("work", [P, 14848])

        def part(at, n):
            return work[:, at:at + n]

        qA, kA, vA = part(0, 512), part(512, 512), part(1024, 512)
        vArow = part(1536, 512).rearrange("p (t c) -> p t c", t=ST)
        biased = part(2048, 1024).rearrange("p (r c) -> p r c", r=2)
        probs = part(3072, 1024).rearrange("p (r c) -> p r c", r=2)
        probsT = part(4096, 1024).rearrange("p (r c) -> p r c", r=2)
        qR, kR, vR = part(5120, 512), part(5632, 512), part(6144, 512)
        vRrow = part(6656, 512).rearrange("p (t c) -> p t c", t=ST)
        gate = part(7168, 512)
        rotc, rots = part(7680, 512), part(8192, 512)
        retp = part(8704, 2560).rearrange("p (h c) -> p h c", h=2)
        centered, squares = part(11264, 512), part(11776, 512)
        gated = part(12288, 512)
        btab = part(12800, 1024).rearrange("p (h c) -> p h c", h=2)
        dtab = part(13824, 1024).rearrange("p (h c) -> p h c", h=2)
        hrow = part(0, 2048).rearrange("p (r c) -> p r c", r=2)
        orow = part(2048, 2048).rearrange("p (r c) -> p r c", r=2)
        junk = part(4096, 1024)
        fT = part(0, FT * SEQ).rearrange("p (t c) -> p t c", t=FT)
        ca = part(11264, 1024).rearrange("p (r c) -> p r c", r=2)
        cb = part(12288, 1024).rearrange("p (r c) -> p r c", r=2)
        oT = part(11264, 2048).rearrange("p (t c) -> p t c", t=4)
        last = part(0, 4096).rearrange("p (s c) -> p s c", s=ST)
        junk2 = part(13312, 512)

        bank = [ctx.enter_context(nc.psum_tensor(f"bank{b}", [P, 512], F32)) for b in range(8)]
        UNIT_BANK = [0, 1, 0, 1, 0, 1, 7]
        S_BANK, T_BANK, YA_BANK, YR_BANK = (2, 3), (4, 5), 6, 7
        O_BANK = [(0, 1), (5, 6), (2, 3), (4, 7)]

        x_loaded = [sem(f"x_loaded{s}") for s in range(ST)]
        raw_loaded = [sem(f"raw_loaded{s}") for s in range(SLOTS)]
        gains_loaded = sem("gains_loaded")
        gains1_loaded = sem("gains1_loaded")
        load_granted, bias_granted = sem("load_granted"), sem("bias_granted")
        gains2_loaded = sem("gains2_loaded")
        gains3_loaded = sem("gains3_loaded")
        small_loaded = sem("small_loaded")
        rot_loaded = sem("rot_loaded")
        btab_loaded, dtab_loaded = sem("btab_loaded"), sem("dtab_loaded")
        bvec_stored = sem("bvec_stored")
        out_stored = sem("out_stored")
        const_set = sem("const_set")
        ident_set = sem("ident_set")
        conv_turned, conv_ready = sem("conv_turned"), sem("conv_ready")
        bvec_made, bvec_ready = sem("bvec_made"), sem("bvec_ready")
        sq_done, ms_done, rstd_done = sem("sq_done"), sem("ms_done"), sem("rstd_done")
        h_rows, h_turned = sem("h_rows"), sem("h_turned")
        h_hi, h_lo = sem("h_hi"), sem("h_lo")
        w_hi, w_lo, unit_done = sem("w_hi"), sem("w_lo"), sem("unit_done")
        evacuated = sem("evacuated")
        swapped, cos_done, sin_done, rotated = sem("swapped"), sem("cos_done"), sem("sin_done"), sem("rotated")
        gate_exp, gate_plus, gate_inv, gate_ready = sem("gate_exp"), sem("gate_plus"), sem("gate_inv"), sem("gate_ready")
        vA_turned, vA_ready = sem("vA_turned"), sem("vA_ready")
        a_scores, a_biased, a_exp, a_inv = sem("a_scores"), sem("a_biased"), sem("a_exp"), sem("a_inv")
        a_probs, a_turned, a_probsT, a_pv = sem("a_probs"), sem("a_turned"), sem("a_probsT"), sem("a_pv")
        a_yhi, a_ylo = sem("a_yhi"), sem("a_ylo")
        vR_turned, vR_ready = sem("vR_turned"), sem("vR_ready")
        r_scores, r_decayed, r_pv = sem("r_scores"), sem("r_decayed"), sem("r_pv")
        r_sum, r_neg, r_centered, r_sq = sem("r_sum"), sem("r_neg"), sem("r_centered"), sem("r_sq")
        r_var, r_ms, r_rstd, r_normed = sem("r_var"), sem("r_ms"), sem("r_rstd"), sem("r_normed")
        r_turned, r_gated, r_yhi, r_ylo = sem("r_turned"), sem("r_gated"), sem("r_yhi"), sem("r_ylo")
        o_done = sem("o_done")
        o_sq, o_sum, o_ms, o_rstd = sem("o_sq"), sem("o_sum"), sem("o_ms"), sem("o_rstd")
        o_scaled, x_added = sem("o_scaled"), sem("x_added")
        tap2, tap1, tap0 = sem("tap2"), sem("tap1"), sem("tap0")
        gelu_done, f_ready = sem("gelu_done"), sem("f_ready")
        f_hi, f_lo = sem("f_hi"), sem("f_lo")
        oT_act, oT_dve, oT_turned = sem("oT_act"), sem("oT_dve"), sem("oT_turned")
        block = ctx.enter_context(nc.Block())

        w_in_v = w_in[0].rearrange("(k p) n -> p k n", p=P)
        w_up_v = w_up[0].rearrange("(k p) n -> p k n", p=P)
        w_out_v = w_out[0].rearrange("(k p) n -> p k n", p=P)
        w_down_v = w_down[0].rearrange("(k p) n -> p k n", p=P)
        bias_dram = nc.dram_tensor("bias_vectors", (HEADS, VEC), F32, kind="Internal")

        def width(t):
            return P * (t + 1)

        def packed(mt):
            return P * mt * (mt + 1) // 2

        def f_part(c):
            return slice(512 * c, 512 * c + 512)

        @block.sync
        def _(sp):
            for s in range(ST):
                sp.dma_start(xs[:, s, :], x[0, s * P:(s + 1) * P, :]).then_inc(x_loaded[s], 16)
                if s == 0:
                    sp.dma_start(gains[:, 0, :], norm_mix_pre[0].partition_broadcast(P)).then_inc(gains_loaded, 16)
            sp.dma_start(gains[:, 1, :], norm_mix_post[0].partition_broadcast(P)).then_inc(gains1_loaded, 16)

            def load(n, i, per_turn, source, k_major=True):
                c = slot_of(n)
                if not (isinstance(i, int) and freed_at(n + i * per_turn) == 0):
                    sp.wait_ge(w_lo, at_turn(freed_at, n, i, per_turn))
                    if not isinstance(i, int):
                        sp.sem_inc(load_granted, 1)
                dst = raw[:, c, :]
                if k_major:
                    dst = dst.rearrange("p (k n) -> p k n", n=source.shape[-1])
                sp.dma_start(dst, source).then_inc(raw_loaded[c], 16)

            def load_turn(i):
                for j in range(NU):
                    load(j, i, NU, w_in_v[:, :, bass.ds(GROUPS[j] * DMIX + i * P, P)])

            load_turn(0)
            with sp.Fori(1, PAIRS) as i:
                load_turn(i)
            for n in range(2 * KT):
                load(OUT0 + n, 0, 0, w_out_v[:, n % KT, :], k_major=False)
            with sp.Fori(0, SWEEP) as i:
                for j in range(4):
                    side, half = j % 2, j // 2
                    load(UP0 + j, i, 4, w_up_v[:, :, bass.ds(side * DFF + half * P + i * (2 * P), P)])
            for sweep in range(2):
                cols = slice(sweep * 512, sweep * 512 + 512)
                first = DOWN0 + sweep * SWEEP
                with sp.Fori(0, SWEEP // 2) as i:
                    for q in range(2):
                        load(first + q, i, 2, w_down_v[:, bass.ds(2 * q + 4 * i, 2), cols])
                load(first + SWEEP - 1, 0, 0, w_down_v[:, FT - 2:FT, cols])
            for s in range(ST):
                for half in range(2):
                    sp.wait_ge(x_added, ST + 2 * s + half + 1)
                    sp.dma_start(out[0, s * P:(s + 1) * P, half * 512:half * 512 + 512],
                                 last[:, s, half * 512:half * 512 + 512]).then_inc(out_stored, 16)
            sp.wait_ge(out_stored, 16 * 2 * ST)

        @block.gpsimd
        def _(pool):
            pool.memset(neghalf[:], -0.5).then_inc(const_set, 1)
            pool.wait_ge(const_set, 1)
            pool.memset(relb[BUCKETS:BUCKETS + 1, :], -1e30).then_inc(const_set, 1)
            pool.wait_ge(const_set, 2)
            pool.memset(ident[:], 0.0).then_inc(ident_set, 1)
            pool.dma_start(relb[0:BUCKETS, :], rel_bias).then_inc(small_loaded, 16)
            pool.dma_start(oneh[:], onehot).then_inc(small_loaded, 16)
            pool.dma_start(convrows[:, 0:3, :], conv_w[0].rearrange("j (t p) -> t j p", p=P)).then_inc(small_loaded, 16)
            pool.dma_start(convrows[:, 3, :], conv_b[0].rearrange("(t p) -> t p", p=P)).then_inc(small_loaded, 16)
            pool.wait_ge(ident_set, 1)
            pool.affine_select(out=ident[:], in_=ident[:], compare_op=ALU.not_equal, fill=1.0, base=0,
                               pattern=[[-1, P]], channel_multiplier=1).then_inc(ident_set, 1)
            pool.dma_start(rot[:], rotary).then_inc(rot_loaded, 16)
            pool.wait_ge(ident_set, 2)

            def row_rstd(t, src):
                nc.gpsimd.tensor_scalar(meansq[:, t:t + 1], src, 1.0 / D, EPS, ALU.mult, ALU.add).then_inc(ms_done, 1)
                pool.wait_ge(ms_done, t + 1)
                nc.gpsimd.tensor_tensor(rstd[:, t:t + 1], meansq[:, t:t + 1], neghalf[:, 0:1], ALU.pow).then_inc(rstd_done, 1)

            def out_rstd(t):
                pool.wait_ge(o_sq, 2 * t + 2 if t < ST else 2 * ST + ST + (t - ST) + 1)
                nc.gpsimd.tensor_tensor(meansq[:, 8 + t:9 + t], osum[:, t, 0:1], osum[:, t, 1:2], ALU.add).then_inc(o_sum, 1)
                pool.wait_ge(o_sum, t + 1)
                nc.gpsimd.tensor_scalar(sumsq[:, 8 + t:9 + t], meansq[:, 8 + t:9 + t], 1.0 / D, EPS,
                                        ALU.mult, ALU.add).then_inc(o_ms, 1)
                pool.wait_ge(o_ms, t + 1)
                nc.gpsimd.tensor_tensor(rstd[:, 8 + t:9 + t], sumsq[:, 8 + t:9 + t], neghalf[:, 0:1],
                                        ALU.pow).then_inc(o_rstd, 1)

            for s in range(ST):
                pool.wait_ge(sq_done, s + 1)
                row_rstd(s, sumsq[:, s:s + 1])
            pool.wait_ge(bvec_ready, 2)
            pool.dma_start(bias_dram[:, :], bvec[:]).then_inc(bvec_stored, 16)
            pool.wait_ge(bvec_stored, 16)

            def group_rstd(k):
                pool.wait_ge(r_var, k + 1)
                nc.gpsimd.tensor_scalar(gms[:], gvar[:], 1.0 / HD, EPS, ALU.mult, ALU.add).then_inc(r_ms, 1)
                pool.wait_ge(r_ms, k + 1)
                nc.gpsimd.tensor_tensor(grstd[:], gms[:], neghalf[:], ALU.pow).then_inc(r_rstd, 1)

            for i in range(PAIRS):
                if i:
                    pool.wait_ge(a_biased, 8 * i)
                pool.dma_start(btab, window(bias_dram, 2 * i, 2)).then_inc(btab_loaded, 16)
                if i:
                    group_rstd(i - 1)
                    pool.wait_ge(r_decayed, 8 * i)
                pool.dma_start(dtab, window(decay.tensor, 2 * i, 2)).then_inc(dtab_loaded, 16)
                for side, dst in ((0, kR[:, ::-1]), (1, qR)):
                    pool.wait_ge(sin_done, 2 * i + side + 1)
                    if i:
                        pool.wait_ge(r_scores, 8 * i)
                    nc.gpsimd.tensor_tensor(dst, rotc, rots, ALU.add).then_inc(rotated, 1)
            group_rstd(PAIRS - 1)
            pool.wait_ge(h_rows, ST)
            pool.dma_start(gains[:, 0, :], norm_ffn_pre[0].partition_broadcast(P)).then_inc(gains2_loaded, 16)
            for pair in ((0, 1), (2, 3)):
                for s in pair:
                    out_rstd(s)
                for s in pair:
                    pool.wait_ge(sq_done, ST + s + 1)
                    row_rstd(ST + s, sumsq[:, ST + s:ST + s + 1])
            pool.wait_ge(o_scaled, 2 * ST)
            pool.dma_start(gains[:, 1, :], norm_ffn_post[0].partition_broadcast(P)).then_inc(gains3_loaded, 16)
            for s in range(ST):
                out_rstd(ST + s)

        @block.tensor
        def _(pe):
            def three(dst, st_hi, st_lo, mv_hi, mv_lo, p, start, stop):
                st, mv = ((st_hi, mv_hi), (st_hi, mv_lo), (st_lo, mv_hi))[p]
                return nc.tensor.matmul(dst, st, mv, start=start, stop=stop)

            def turn_rows(t):
                banks = O_BANK[t % ST] if t >= ST else (2 * (t % 2), 2 * (t % 2) + 1)
                pe.wait_ge(h_rows, t + 1)
                for half in range(2):
                    if 2 <= t < ST:
                        pe.wait_ge(h_lo, 2 * (t - 2) + half + 1)
                    for k in range(4):
                        c = (4 * half + k) * P
                        ins = nc.tensor.transpose(bank[banks[half]][:, k * P:(k + 1) * P],
                                                  hrow[:, t % 2, c:c + P], ident[:])
                    ins.then_inc(h_turned, 1)

            def column_unit(n, i, per_turn, dst, m0, m1):
                c = slot_of(n)
                for m in range(m0, m1):
                    k, p = divmod(m, 3)
                    cols = slice(k * P, (k + 1) * P)
                    ins = three(dst, ws[:, c, 0, cols], ws[:, c, 1, cols], hT[:, 0, k, :], hT[:, 1, k, :], p,
                                m == 0, m == 23)
                if m1 == 24:
                    ins.then_inc(unit_done, 1)

            def project(i, j, m0, m1):
                if m0 == 0:
                    pe.wait_ge(w_lo, at_turn(lambda n: n + 1, j, i, NU))
                    first = isinstance(i, int) and i == 0
                    if j == 0 and not first:
                        pe.wait_ge(cos_done, 2 * i)
                    if j == 1 and not first:
                        pe.wait_ge(evacuated, 4 * i)
                    if j in (2, 3, 4):
                        pe.wait_ge(evacuated, 4 * i + j - 1)
                    if j == 5:
                        pe.wait_ge(cos_done, 2 * i + 1)
                    if j == 6 and not first:
                        pe.wait_ge(r_gated, i * 1)
                column_unit(j, i, NU, bank[UNIT_BANK[j]][:], m0, m1)

            def ret_values(k):
                pe.wait_ge(evacuated, 4 * k + 4)
                pe.wait_ge(a_probsT, 8 * k + 8)
                for t in range(ST):
                    ins = nc.tensor.transpose(bank[T_BANK[0]][:, t * P:(t + 1) * P], vR[:, t * P:(t + 1) * P], ident[:])
                ins.then_inc(vR_turned, 1)

            def ret_scores(k, u):
                h, mt = u // 4, 3 - u % 4
                if u == 0:
                    pe.wait_ge(rotated, 2 * k + 2)
                    pe.wait_ge(a_biased, 8 * k + 8)
                if u >= 2:
                    pe.wait_ge(r_decayed, 8 * k + u - 1)
                rows = slice(HD * h, HD * h + HD)
                nc.tensor.matmul(bank[S_BANK[u % 2]][:, 0:width(mt)], kR[rows, mt * P:(mt + 1) * P],
                                 qR[rows, SEQ - width(mt):SEQ], start=True, stop=True).then_inc(r_scores, 1)

            def ret_mix(k, u):
                h, nt = u // 4, u % 4
                if u == 0:
                    pe.wait_ge(vR_ready, 1 * k + 1)
                    pe.wait_ge(gate_ready, 1 * k + 1)
                pe.wait_ge(r_decayed, 8 * k + u + 1)
                for mt in range(3 - nt, 4):
                    c = packed(mt) + nt * P - (SEQ - width(mt))
                    ins = nc.tensor.matmul(bank[YR_BANK][:, (2 * nt + h) * HD:(2 * nt + h + 1) * HD],
                                           retp[:, h, c:c + P], vRrow[:, mt, HD * h:HD * h + HD],
                                           start=mt == 3 - nt, stop=mt == 3)
                if u == 7:
                    ins.then_inc(r_pv, 1)

            def ret_turn_out(k):
                pe.wait_ge(r_normed, 1 * k + 1)
                for t in range(ST):
                    ins = nc.tensor.transpose(bank[YR_BANK][:, t * P:(t + 1) * P],
                                              centered[:, t * P:(t + 1) * P], ident[:])
                ins.then_inc(r_turned, 1)

            def moba_values(i):
                pe.wait_ge(evacuated, 4 * i + 3)
                for t in range(ST):
                    ins = nc.tensor.transpose(bank[T_BANK[1]][:, t * P:(t + 1) * P], vA[:, t * P:(t + 1) * P], ident[:])
                ins.then_inc(vA_turned, 1)

            def moba_scores(i, u, first):
                h, qt = u // 4, u % 4
                if u < 2 and not first:
                    pe.wait_ge(r_decayed, 8 * i)
                if u >= 2:
                    pe.wait_ge(a_biased, 8 * i + u - 1)
                rows = slice(HD * h, HD * h + HD)
                nc.tensor.matmul(bank[S_BANK[u % 2]][:, 0:width(qt)], qA[rows, qt * P:(qt + 1) * P],
                                 kA[rows, SEQ - width(qt):SEQ], start=True, stop=True).then_inc(a_scores, 1)

            def moba_turn(i, u):
                qt = u % 4
                pe.wait_ge(a_probs, 8 * i + u + 1)
                if u < 2:
                    pe.wait_ge(vA_ready, 1 * i + 1)
                else:
                    pe.wait_ge(a_probsT, 8 * i + u - 1)
                for t in range(qt + 1):
                    ins = nc.tensor.transpose(bank[T_BANK[u % 2]][:, t * P:(t + 1) * P],
                                              probs[:, u % 2, t * P:(t + 1) * P], ident[:])
                ins.then_inc(a_turned, 1)

            def moba_mix(i, u, first):
                h, qt = u // 4, u % 4
                if u == 0 and not first:
                    pe.wait_ge(a_ylo, 1 * i)
                pe.wait_ge(a_probsT, 8 * i + u + 1)
                for t in range(qt + 1):
                    ins = nc.tensor.matmul(bank[YA_BANK][HD * h:HD * h + HD, qt * P:(qt + 1) * P],
                                           vArow[:, 3 - qt + t, HD * h:HD * h + HD],
                                           probsT[:, u % 2, t * P:(t + 1) * P], start=t == 0, stop=t == qt)
                ins.then_inc(a_pv, 1)

            def mixer_turn(i, first):
                for r in range(9):
                    project(i, r // 3, 8 * (r % 3), 8 * (r % 3) + 8)
                    if not first:
                        if r == 0:
                            ret_values(i - 1)
                        if r >= 2:
                            ret_mix(i - 1, r - 2)
                        if r < 8:
                            ret_scores(i - 1, r)
                for u in range(12):
                    project(i, 3 + u // 3, 8 * (u % 3), 8 * (u % 3) + 8)
                    if u == 0:
                        if not first:
                            ret_mix(i - 1, 7)
                        moba_values(i)
                    if u == 5 and not first:
                        ret_turn_out(i - 1)
                    if 3 <= u < 11:
                        moba_mix(i, u - 3, first)
                    if 2 <= u < 10:
                        moba_turn(i, u - 2)
                    if u < 8:
                        moba_scores(i, u, first)

            pe.wait_ge(small_loaded, 64)
            pe.wait_ge(ident_set, 2)
            pe.wait_ge(const_set, 2)
            for j in range(4):
                ins = nc.tensor.transpose(bank[5][:, j * 2 * FT:(j + 1) * 2 * FT], convrows[:, j, :],
                                          ident[0:2 * FT, 0:2 * FT])
            ins.then_inc(conv_turned, 1)
            for b, lo, hi in ((6, 0, 512), (7, 512, VEC)):
                ins = nc.tensor.matmul(bank[b][0:HEADS, 0:hi - lo], relb[:], oneh[:, lo:hi], start=True, stop=True)
            ins.then_inc(bvec_made, 1)
            for s in range(ST):
                turn_rows(s)
            pe.wait_ge(h_lo, 2 * ST)
            pe.wait_ge(bvec_ready, 2)
            pe.wait_ge(conv_ready, 1)
            mixer_turn(0, True)
            with pe.Fori(1, PAIRS) as i:
                mixer_turn(i, False)

            def out_rows(pass_, m0, m1):
                for m in range(m0, m1):
                    k, r = divmod(m, 12)
                    n = OUT0 + pass_ * KT + k
                    s, half, p = 2 * pass_ + r // 6, r // 3 % 2, r % 3
                    if r == 0:
                        pe.wait_ge(w_lo, n + 1)
                        if pass_ == 0 and k < PAIRS:
                            pe.wait_ge(a_ylo, k + 1)
                        if pass_ == 0 and k >= PAIRS:
                            pe.wait_ge(r_ylo, k - PAIRS + 1)
                    rows = slice(s * P, (s + 1) * P)
                    c = slot_of(n)
                    ins = three(bank[O_BANK[s][half]][:], yT[:, 0, k, rows], yT[:, 1, k, rows],
                                ws[:, c, 0, half * 512:half * 512 + 512], ws[:, c, 1, half * 512:half * 512 + 512],
                                p, k == 0 and p == 0, k == KT - 1 and p == 2)
                    if r == 11:
                        ins.then_inc(unit_done, 1)
                if m1 == 96:
                    pass

            k = PAIRS - 1
            pe.wait_ge(cos_done, 2 * PAIRS)
            pe.wait_ge(evacuated, 4 * PAIRS)
            for r in range(10):
                if r == 0:
                    ret_values(k)
                if r >= 2:
                    ret_mix(k, r - 2)
                if r < 8:
                    ret_scores(k, r)
                if r == 0:
                    pe.wait_ge(a_ylo, PAIRS)
                out_rows(0, 5 * r, 5 * r + 5)
            out_rows(0, 50, 84)
            ret_turn_out(k)
            out_rows(0, 84, 96)
            pe.wait_ge(r_gated, PAIRS)
            pe.wait_ge(r_decayed, 8 * PAIRS)
            pe.wait_ge(vR_ready, PAIRS)
            for k in range(KT):
                out_rows(1, 12 * k, 12 * k + 12)
                if k == 4:
                    turn_rows(ST)
                if k == 6:
                    turn_rows(ST + 1)
            turn_rows(ST + 2)
            turn_rows(ST + 3)

            pe.wait_ge(h_lo, 4 * ST)
            def up_turn(i, first):
                for j in range(4):
                    pe.wait_ge(w_lo, 4 * i + (UP0 + j + 1))
                    if not first:
                        pe.wait_ge(tap0, 4 * i + (j - 3))
                    column_unit(UP0 + j, i, 4, bank[j][:], 0, 24)
            up_turn(0, True)
            with pe.Fori(1, SWEEP) as i:
                up_turn(i, False)

            def down_unit(sweep, n0, q, i, start, stop):
                c = slot_of(n0 + q)
                pe.wait_ge(w_lo, 2 * i + (n0 + q + 1))
                pe.wait_ge(f_lo, 4 * i + (2 * (n0 - DOWN0 + q) + 2))
                for kk in range(2):
                    for dt in range(4):
                        cols = slice(kk * 512 + dt * P, kk * 512 + (dt + 1) * P)
                        for p in range(3):
                            ins = three(bank[(4 if sweep == 0 else 0) + dt][:], ws[:, c, 0, cols], ws[:, c, 1, cols],
                                        yT[:, 0, 2 * c + kk, :], yT[:, 1, 2 * c + kk, :], p,
                                        start and kk == 0 and p == 0, stop and kk == 1 and p == 2)
                ins.then_inc(unit_done, 1)

            def turn_down(sweep):
                pe.wait_ge(oT_act, 2 * sweep + 2)
                pe.wait_ge(oT_dve, 2 * sweep + 2)
                for s in range(ST):
                    for dt in range(4):
                        ins = nc.tensor.transpose(bank[(4 if sweep == 0 else 0) + s][:, dt * P:(dt + 1) * P],
                                                  oT[:, dt, s * P:(s + 1) * P], ident[:])
                    ins.then_inc(oT_turned, 1)

            for sweep in range(2):
                first = DOWN0 + sweep * SWEEP
                if sweep == 1:
                    pe.wait_ge(tap0, 2 * FT)
                for q in range(2):
                    down_unit(sweep, first, q, 0, q == 0, False)
                with pe.Fori(1, SWEEP // 2) as i:
                    for q in range(2):
                        down_unit(sweep, first, q, i, False, False)
                if sweep == 1:
                    turn_down(0)
                down_unit(sweep, first + SWEEP - 1, 0, 0, False, True)
            turn_down(1)

        @block.scalar
        def _(act):
            def split_hi(n, i=0, per_turn=0):
                c = slot_of(n)
                act.wait_ge(raw_loaded[c], at_turn(lambda m: 16 * loads_of_slot(m), n, i, per_turn)
                            if n < DOWN0 else 16 * (i * 1) + 16 * loads_of_slot(n))
                if not (isinstance(i, int) and freed_at(n + i * per_turn) == 0):
                    act.wait_ge(unit_done, at_turn(freed_at, n, i, per_turn))
                nc.scalar.activation(ws[:, c, 0, :], raw[:, c, :], ACT.Copy).then_inc(w_hi, 1)

            def h_evacuate(t):
                banks = O_BANK[t % ST] if t >= ST else (2 * (t % 2), 2 * (t % 2) + 1)
                s = t % ST
                for half in range(2):
                    act.wait_ge(h_turned, 2 * t + half + 1)
                    nc.scalar.activation(hT[:, 0, 4 * half:4 * half + 4, s * P:(s + 1) * P],
                                         bank[banks[half]][:].rearrange("p (k c) -> p k c", k=4),
                                         ACT.Copy).then_inc(h_hi, 1)

            def row_squares(t):
                if t:
                    act.wait_ge(sq_done, t)
                nc.scalar.activation(junk, xs[:, t % ST, :], ACT.Square, accum_out=sumsq[:, t:t + 1]).then_inc(sq_done, 1)

            act.wait_ge(conv_turned, 1)
            nc.scalar.activation(conv[:], bank[5][:, 0:8 * FT], ACT.Copy).then_inc(conv_ready, 1)
            act.wait_ge(bvec_made, 1)
            for b, lo, hi in ((6, 0, 512), (7, 512, VEC)):
                nc.scalar.activation(bvec[:, lo:hi], bank[b][0:HEADS, 0:hi - lo], ACT.Copy, scale=8.0).then_inc(bvec_ready, 1)
            for s in range(ST):
                act.wait_ge(x_loaded[s], 16)
                row_squares(s)
            split_hi(0)
            split_hi(1)
            for s in range(ST):
                h_evacuate(s)

            def evacuate(i, j, dst, first):
                act.wait_ge(unit_done, at_turn(lambda n: n + 1, j, i, NU))
                nc.scalar.activation(dst, bank[UNIT_BANK[j]][:], ACT.Copy).then_inc(evacuated, 1)

            def swap_halves(i, j, first):
                act.wait_ge(unit_done, at_turn(lambda n: n + 1, j, i, NU))
                if j == QR or not first:
                    act.wait_ge(rotated, 2 * i + (j - KR))
                for b in range(4):
                    src = 32 * (b ^ 1)
                    ins = nc.scalar.activation(rots[32 * b:32 * b + 32, :], bank[UNIT_BANK[j]][src:src + 32, :], ACT.Copy)
                ins.then_inc(swapped, 1)

            def gate_exponent(k):
                act.wait_ge(unit_done, at_turn(lambda n: n + 1, GR, k, NU))
                nc.scalar.activation(gate, bank[UNIT_BANK[GR]][:], ACT.Exp, scale=-1.0).then_inc(gate_exp, 1)

            def mixer_turn(i, first):
                for r in range(9):
                    if r == 0 and not first:
                        gate_exponent(i - 1)
                        act.wait_ge(vR_turned, 1 * i)
                        nc.scalar.activation(vRrow, bank[T_BANK[0]][:].rearrange("p (t c) -> p t c", t=ST),
                                             ACT.Copy).then_inc(vR_ready, 1)
                    if r == 3:
                        if not first:
                            act.wait_ge(a_scores, 8 * i)
                        evacuate(i, KA, kA[:, ::-1], first)
                    if r == 6:
                        evacuate(i, QA, qA, first)
                    if r % 3 == 1:
                        split_hi(r // 3 + 2, i, NU)
                for u in range(12):
                    if u == 0:
                        evacuate(i, VA, vA[:, ::-1], first)
                    if u == 3:
                        swap_halves(i, KR, first)
                    if u == 6:
                        swap_halves(i, QR, first)
                    if u == 9:
                        evacuate(i, VR, vR[:, ::-1], first)
                    if u == 1:
                        if not first:
                            act.wait_ge(a_pv, 8 * i)
                        act.wait_ge(vA_turned, 1 * i + 1)
                        nc.scalar.activation(vArow, bank[T_BANK[1]][:].rearrange("p (t c) -> p t c", t=ST),
                                             ACT.Copy).then_inc(vA_ready, 1)
                    if u == 2 and not first:
                        act.wait_ge(r_centered, 1 * i)
                        nc.scalar.activation(squares, centered, ACT.Square).then_inc(r_sq, 1)
                    if u < 8:
                        w = width(u % 4)
                        act.wait_ge(a_biased, 8 * i + u + 1)
                        if u >= 2:
                            act.wait_ge(a_turned, 8 * i + u - 1)
                        nc.scalar.activation(probs[:, u % 2, 0:w], biased[:, u % 2, 0:w], ACT.Exp, scale=-1.0,
                                             bias=negmax[:, u:u + 1], accum_out=rowsum[:, u:u + 1]).then_inc(a_exp, 1)
                    if 2 <= u < 10:
                        v = u - 2
                        w = width(v % 4)
                        act.wait_ge(a_turned, 8 * i + v + 1)
                        if v >= 2:
                            act.wait_ge(a_pv, 8 * i + v - 1)
                        nc.scalar.activation(probsT[:, v % 2, 0:w], bank[T_BANK[v % 2]][:, 0:w],
                                             ACT.Copy).then_inc(a_probsT, 1)
                    if u == 6 and not first:
                        act.wait_ge(r_gated, 1 * i)
                        nc.scalar.activation(yT[:, 0, i + (PAIRS - 1), :] if isinstance(i, int)
                                             else yT[:, 0, bass.ds(i + (PAIRS - 1), 1), :].rearrange("p o c -> p (o c)"),
                                             gated, ACT.Copy).then_inc(r_yhi, 1)
                    if u % 3 == 1:
                        split_hi(u // 3 + 5, i, NU)
                act.wait_ge(a_pv, 8 * i + 8)
                nc.scalar.activation(yT[:, 0, i, :] if isinstance(i, int)
                                     else yT[:, 0, bass.ds(i, 1), :].rearrange("p o c -> p (o c)"),
                                     bank[YA_BANK][:], ACT.Copy).then_inc(a_yhi, 1)

            mixer_turn(0, True)
            with act.Fori(1, PAIRS) as i:
                mixer_turn(i, False)

            k = PAIRS - 1
            gate_exponent(k)
            act.wait_ge(vR_turned, PAIRS)
            nc.scalar.activation(vRrow, bank[T_BANK[0]][:].rearrange("p (t c) -> p t c", t=ST), ACT.Copy).then_inc(vR_ready, 1)
            for n in range(2, 7):
                split_hi(OUT0 + n)
            act.wait_ge(r_centered, PAIRS)
            nc.scalar.activation(squares, centered, ACT.Square).then_inc(r_sq, 1)
            split_hi(OUT0 + 7)
            split_hi(OUT0 + 8)
            act.wait_ge(r_gated, PAIRS)
            nc.scalar.activation(yT[:, 0, KT - 1, :], gated, ACT.Copy).then_inc(r_yhi, 1)
            split_hi(OUT0 + 9)

            def out_squares(s):
                for half in range(2):
                    if s or half:
                        act.wait_ge(o_sq, 2 * s + half)
                    nc.scalar.activation(gate, bank[O_BANK[s][half]][:], ACT.Square,
                                         accum_out=osum[:, s, half:half + 1]).then_inc(o_sq, 1)

            def x_squares(s):
                act.wait_ge(x_added, s + 1)
                row_squares(ST + s)

            for k in range(KT):
                if k == 0:
                    act.wait_ge(unit_done, OUT0 + KT)
                    out_squares(0)
                    out_squares(1)
                if k == 2:
                    x_squares(0)
                if k == 3:
                    x_squares(1)
                if k == 5:
                    h_evacuate(ST)
                if k == 7:
                    h_evacuate(ST + 1)
                split_hi(OUT0 + KT + k + 2)
            act.wait_ge(unit_done, UP0)
            out_squares(2)
            out_squares(3)
            for s in (2, 3):
                x_squares(s)
            for s in (2, 3):
                h_evacuate(ST + s)

            def up_post(i, j, first):
                t = 2 * i + ((FT if j % 2 else 0) + j // 2)
                dst = (cb if j % 2 else ca)[:, j // 2, :]
                act.wait_ge(unit_done, 4 * i + (UP0 + j + 1))
                if not first:
                    act.wait_ge(f_ready, 2 * i + (j // 2 - 1))
                def col(tap):
                    c = 2 * FT * tap + t
                    return conv[:, c:c + 1] if isinstance(c, int) else conv[:, bass.ds(c, 1)]
                nc.scalar.activation(dst, bank[j][:], ACT.Identity, scale=col(2), bias=col(3)).then_inc(tap2, 1)
                if j % 2:
                    act.wait_ge(tap0, 4 * i + j)
                    nc.scalar.activation(ca[:, j // 2, :], ca[:, j // 2, :], ACT.Gelu_apprx_tanh).then_inc(gelu_done, 1)

            def f_split_hi(n0, q, i):
                for kk in range(2):
                    k0 = 2 * ((n0 - DOWN0) % SWEEP + q) + kk
                    k = 4 * i + k0
                    src = fT[:, k, :] if isinstance(k, int) else fT[:, bass.ds(k, 1), :].rearrange("p o c -> p (o c)")
                    nc.scalar.activation(yT[:, 0, 2 * slot_of(n0 + q) + kk, :], src, ACT.Copy).then_inc(f_hi, 1)

            def down_hi(n0, q, i):
                c = slot_of(n0 + q)
                act.wait_ge(raw_loaded[c], 16 * i + 16 * loads_of_slot(n0 + q))
                act.wait_ge(unit_done, 2 * i + (n0 + q - 1))
                nc.scalar.activation(ws[:, c, 0, :], raw[:, c, :], ACT.Copy).then_inc(w_hi, 1)
                f_split_hi(n0, q, i)

            for j in range(4):
                split_hi(UP0 + 2 + j)
                up_post(0, j, True)
            with act.Fori(1, SWEEP - 1) as i:
                for j in range(4):
                    split_hi(UP0 + 2 + j, i, 4)
                    up_post(i, j, False)
            for j in range(4):
                if j < 2:
                    split_hi(UP0 + 2 + j, SWEEP - 1, 4)
                else:
                    down_hi(DOWN0, j - 2, 0)
                up_post(SWEEP - 1, j, False)
            for sweep in range(2):
                first = DOWN0 + sweep * SWEEP
                if sweep:
                    for q in range(2):
                        down_hi(first, q, 0)
                    for dt in range(2):
                        act.wait_ge(unit_done, first)
                        nc.scalar.activation(oT[:, dt, :], bank[4 + dt][:], ACT.Copy).then_inc(oT_act, 1)
                with act.Fori(1, SWEEP // 2) as i:
                    for q in range(2):
                        down_hi(first, q, i)
                if sweep == 0:
                    act.wait_ge(f_ready, FT)
                down_hi(first + SWEEP - 1, 0, 0)

            def down_squares(half):
                for s in range(ST):
                    act.wait_ge(oT_turned, ST * half + s + 1)
                    act.wait_ge(o_sq, 2 * ST + ST * half + s)
                    nc.scalar.activation(junk2, bank[(4 if half == 0 else 0) + s][:], ACT.Square,
                                         accum_out=osum[:, ST + s, half:half + 1]).then_inc(o_sq, 1)

            down_squares(0)
            for dt in range(2):
                act.wait_ge(unit_done, LAST_UNIT)
                nc.scalar.activation(oT[:, dt, :], bank[dt][:], ACT.Copy).then_inc(oT_act, 1)
            down_squares(1)

        @block.vector
        def _(dve):
            def f32(ap):
                return ap.bitcast(F32)

            def split_lo(n, i=0, per_turn=0):
                c = slot_of(n)
                dve.wait_ge(w_hi, at_turn(lambda m: m + 1, n, i, per_turn))
                nc.vector.tensor_tensor(ws[:, c, 1, :], raw[:, c, :], f32(ws[:, c, 0, :]), ALU.subtract).then_inc(w_lo, 1)

            def normed_rows(t):
                dve.wait_ge(rstd_done, t + 1)
                if t % ST >= 2:
                    dve.wait_ge(h_turned, 2 * (t - 1))
                nc.vector.scalar_tensor_tensor(hrow[:, t % 2, :], xs[:, t % ST, :], rstd[:, t:t + 1],
                                               gains[:, 0, :], ALU.mult, ALU.mult).then_inc(h_rows, 1)

            def h_low(t):
                banks = O_BANK[t % ST] if t >= ST else (2 * (t % 2), 2 * (t % 2) + 1)
                s = t % ST
                for half in range(2):
                    dve.wait_ge(h_hi, 2 * t + half + 1)
                    cols = (slice(None), slice(4 * half, 4 * half + 4), slice(s * P, (s + 1) * P))
                    nc.vector.tensor_tensor(hT[:, 1, 4 * half:4 * half + 4, s * P:(s + 1) * P],
                                            bank[banks[half]][:].rearrange("p (k c) -> p k c", k=4),
                                            f32(hT[:, 0, 4 * half:4 * half + 4, s * P:(s + 1) * P]),
                                            ALU.subtract).then_inc(h_lo, 1)

            dve.wait_ge(gains_loaded, 16)
            for s in range(ST):
                normed_rows(s)
                if s == 1:
                    split_lo(0)
                if s >= 1:
                    h_low(s - 1)
            h_low(ST - 1)
            split_lo(1)
            dve.wait_ge(rot_loaded, 16)

            def gate_finish(k):
                dve.wait_ge(gate_exp, 1 * k + 1)
                nc.vector.tensor_scalar(gate, gate, 1.0, None, ALU.add).then_inc(gate_plus, 1)
                dve.wait_ge(gate_plus, 1 * k + 1)
                nc.vector.reciprocal(gate, gate).then_inc(gate_inv, 1)
                dve.wait_ge(gate_inv, 1 * k + 1)
                nc.vector.tensor_tensor(gate, bank[UNIT_BANK[GR]][:], gate, ALU.mult).then_inc(gate_ready, 1)

            def ret_decay(k, u):
                h, mt = u // 4, 3 - u % 4
                if u == 0:
                    dve.wait_ge(dtab_loaded, 16 * k + 16)
                dve.wait_ge(r_scores, 8 * k + u + 1)
                nc.vector.tensor_tensor(retp[:, h, packed(mt):packed(mt) + width(mt)],
                                        bank[S_BANK[u % 2]][:, 0:width(mt)], dtab[:, h, 0:width(mt)],
                                        ALU.mult).then_inc(r_decayed, 1)

            def grouped(ap):
                return ap.rearrange("p (g e) -> p g e", e=HD)

            def spread(ap):
                return ap.unsqueeze(2).to_broadcast([P, HEADS, HD])

            def ret_center(k):
                dve.wait_ge(r_pv, 1 * k + 1)
                nc.vector.tensor_reduce(gsum[:], grouped(bank[YR_BANK][:]), AX.X, ALU.add).then_inc(r_sum, 1)
                dve.wait_ge(r_sum, 1 * k + 1)
                nc.vector.tensor_scalar(gneg[:], gsum[:], -1.0 / HD, None, ALU.mult).then_inc(r_neg, 1)
                dve.wait_ge(r_neg, 1 * k + 1)
                nc.vector.tensor_tensor(grouped(centered), grouped(bank[YR_BANK][:]), spread(gneg[:]),
                                        ALU.add).then_inc(r_centered, 1)

            def ret_variance(k):
                dve.wait_ge(r_sq, 1 * k + 1)
                nc.vector.tensor_reduce(gvar[:], grouped(squares), AX.X, ALU.add).then_inc(r_var, 1)

            def ret_norm(k):
                dve.wait_ge(r_rstd, 1 * k + 1)
                nc.vector.tensor_tensor(grouped(centered), grouped(centered), spread(grstd[:]),
                                        ALU.mult).then_inc(r_normed, 1)

            def ret_gate(k):
                dve.wait_ge(r_turned, 1 * k + 1)
                nc.vector.tensor_tensor(gated, bank[YR_BANK][:], gate, ALU.mult).then_inc(r_gated, 1)

            def y_slice(half, k):
                return (yT[:, half, k, :] if isinstance(k, int)
                        else yT[:, half, bass.ds(k, 1), :].rearrange("p o c -> p (o c)"))

            def ret_low(k):
                dve.wait_ge(r_yhi, 1 * k + 1)
                nc.vector.tensor_tensor(y_slice(1, k + PAIRS), gated, f32(y_slice(0, k + PAIRS)),
                                        ALU.subtract).then_inc(r_ylo, 1)

            def bias_and_max(i, u, first):
                h, w = u // 4, width(u % 4)
                if u == 0:
                    dve.wait_ge(btab_loaded, 16 * i + 16)
                dve.wait_ge(a_scores, 8 * i + u + 1)
                if u >= 2:
                    dve.wait_ge(a_exp, 8 * i + u - 1)
                if not first:
                    dve.sem_inc(bias_granted, 1)
                nc.vector.tensor_tensor_reduce(out=biased[:, u % 2, 0:w], in0=bank[S_BANK[u % 2]][:, 0:w],
                                               in1=btab[:, h, 0:w], scale=-0.125, scalar=3.0e38, op0=ALU.add,
                                               op1=ALU.min, accum_out=negmax[:, u:u + 1]).then_inc(a_biased, 1)

            def normalise(i, u):
                w = width(u % 4)
                dve.wait_ge(a_exp, 8 * i + u + 1)
                nc.vector.reciprocal(rowinv[:, u:u + 1], rowsum[:, u:u + 1]).then_inc(a_inv, 1)
                dve.wait_ge(a_inv, 8 * i + u + 1)
                nc.vector.tensor_scalar(probs[:, u % 2, 0:w], probs[:, u % 2, 0:w], rowinv[:, u:u + 1], None,
                                        ALU.mult).then_inc(a_probs, 1)

            def rotate(i, j):
                side = j - KR
                dve.wait_ge(swapped, 2 * i + side + 1)
                nc.vector.tensor_tensor(rotc, bank[UNIT_BANK[j]][:], rot[:, 0, :], ALU.mult).then_inc(cos_done, 1)
                nc.vector.tensor_tensor(rots, rots, rot[:, 1, :], ALU.mult).then_inc(sin_done, 1)

            def mixer_turn(i, first):
                for r in range(9):
                    if r == 1 and not first:
                        gate_finish(i - 1)
                    if r < 8 and not first:
                        ret_decay(i - 1, r)
                    if r % 3 == 1:
                        split_lo(r // 3 + 2, i, NU)
                for u in range(12):
                    if 1 <= u < 9:
                        normalise(i, u - 1)
                    if u < 8:
                        bias_and_max(i, u, first)
                    if not first:
                        if u == 1:
                            ret_center(i - 1)
                        if u == 3:
                            ret_variance(i - 1)
                        if u == 4:
                            ret_norm(i - 1)
                        if u == 6:
                            ret_gate(i - 1)
                        if u == 7:
                            ret_low(i - 1)
                    if u % 3 == 1:
                        split_lo(u // 3 + 5, i, NU)
                    if u == 4:
                        rotate(i, KR)
                    if u == 7:
                        rotate(i, QR)
                dve.wait_ge(a_yhi, 1 * i + 1)
                nc.vector.tensor_tensor(y_slice(1, i), bank[YA_BANK][:], f32(y_slice(0, i)), ALU.subtract).then_inc(a_ylo, 1)

            mixer_turn(0, True)
            with dve.Fori(1, PAIRS) as i:
                mixer_turn(i, False)

            k = PAIRS - 1
            gate_finish(k)
            for r in range(8):
                ret_decay(k, r)
                if r in (1, 3, 5, 6):
                    split_lo(OUT0 + 2 + (1, 3, 5, 6).index(r))
            split_lo(OUT0 + 6)
            ret_center(k)
            ret_variance(k)
            ret_norm(k)
            split_lo(OUT0 + 7)
            split_lo(OUT0 + 8)
            ret_gate(k)
            ret_low(k)
            split_lo(OUT0 + 9)

            def out_residual(s):
                if s == 0:
                    dve.wait_ge(gains1_loaded, 16)
                dve.wait_ge(o_rstd, s + 1)
                if s >= 2:
                    dve.wait_ge(x_added, s - 1)
                for half in range(2):
                    nc.vector.scalar_tensor_tensor(orow[:, s % 2, half * 512:half * 512 + 512], bank[O_BANK[s][half]][:],
                                                   rstd[:, 8 + s:9 + s], gains[:, 1, half * 512:half * 512 + 512],
                                                   ALU.mult, ALU.mult).then_inc(o_scaled, 1)
                dve.wait_ge(o_scaled, 2 * s + 2)
                nc.vector.tensor_tensor(xs[:, s, :], xs[:, s, :], orow[:, s % 2, :], ALU.add).then_inc(x_added, 1)

            dve.wait_ge(gains2_loaded, 16)
            for k in range(KT):
                if k == 0:
                    out_residual(0)
                if k == 1:
                    out_residual(1)
                if k == 3:
                    normed_rows(ST)
                if k == 4:
                    normed_rows(ST + 1)
                if k == 5:
                    h_low(ST)
                if k == 7:
                    h_low(ST + 1)
                split_lo(OUT0 + KT + k + 2)
            out_residual(2)
            out_residual(3)
            normed_rows(ST + 2)
            normed_rows(ST + 3)
            h_low(ST + 2)
            h_low(ST + 3)

            def up_post(i, j):
                t = 2 * i + ((FT if j % 2 else 0) + j // 2)
                c = (cb if j % 2 else ca)[:, j // 2, :]

                def col(tap):
                    a = 2 * FT * tap + t
                    return conv[:, a:a + 1] if isinstance(a, int) else conv[:, bass.ds(a, 1)]
                dve.wait_ge(tap2, 4 * i + (j + 1))
                nc.vector.scalar_tensor_tensor(c[:, 1:SEQ], bank[j][:, 0:SEQ - 1], col(1), c[:, 1:SEQ],
                                               ALU.mult, ALU.add).then_inc(tap1, 1)
                dve.wait_ge(tap1, 4 * i + (j + 1))
                nc.vector.scalar_tensor_tensor(c[:, 2:SEQ], bank[j][:, 0:SEQ - 2], col(0), c[:, 2:SEQ],
                                               ALU.mult, ALU.add).then_inc(tap0, 1)
                if j % 2:
                    pair = 2 * i + j // 2
                    dst = (fT[:, pair, :] if isinstance(pair, int)
                           else fT[:, bass.ds(pair, 1), :].rearrange("p o c -> p (o c)"))
                    dve.wait_ge(gelu_done, 2 * i + (j // 2 + 1))
                    dve.wait_ge(tap0, 4 * i + (j + 1))
                    nc.vector.tensor_tensor(dst, ca[:, j // 2, :], cb[:, j // 2, :], ALU.mult).then_inc(f_ready, 1)

            def down_lo(n0, q, i):
                c = slot_of(n0 + q)
                dve.wait_ge(w_hi, 2 * i + (n0 + q + 1))
                nc.vector.tensor_tensor(ws[:, c, 1, :], raw[:, c, :], f32(ws[:, c, 0, :]), ALU.subtract).then_inc(w_lo, 1)
                for kk in range(2):
                    k = 4 * i + (2 * ((n0 - DOWN0) % SWEEP + q) + kk)
                    src = fT[:, k, :] if isinstance(k, int) else fT[:, bass.ds(k, 1), :].rearrange("p o c -> p (o c)")
                    dve.wait_ge(f_hi, 4 * i + (2 * (n0 - DOWN0 + q) + kk + 1))
                    nc.vector.tensor_tensor(yT[:, 1, 2 * c + kk, :], src, f32(yT[:, 0, 2 * c + kk, :]),
                                            ALU.subtract).then_inc(f_lo, 1)

            for j in range(4):
                split_lo(UP0 + 2 + j)
                up_post(0, j)
            with dve.Fori(1, SWEEP - 1) as i:
                for j in range(4):
                    split_lo(UP0 + 2 + j, i, 4)
                    up_post(i, j)
            for j in range(4):
                if j < 2:
                    split_lo(UP0 + 2 + j, SWEEP - 1, 4)
                else:
                    down_lo(DOWN0, j - 2, 0)
                up_post(SWEEP - 1, j)
            for sweep in range(2):
                first = DOWN0 + sweep * SWEEP
                if sweep:
                    for q in range(2):
                        down_lo(first, q, 0)
                    for dt in range(2, 4):
                        dve.wait_ge(unit_done, first)
                        nc.vector.tensor_copy(oT[:, dt, :], bank[4 + dt][:]).then_inc(oT_dve, 1)
                with dve.Fori(1, SWEEP // 2) as i:
                    for q in range(2):
                        down_lo(first, q, i)
                down_lo(first + SWEEP - 1, 0, 0)
            for dt in range(2, 4):
                dve.wait_ge(unit_done, LAST_UNIT)
                nc.vector.tensor_copy(oT[:, dt, :], bank[dt][:]).then_inc(oT_dve, 1)
            dve.wait_ge(gains3_loaded, 16)
            for s in range(ST):
                dve.wait_ge(o_rstd, ST + s + 1)
                for half in range(2):
                    cols = slice(half * 512, half * 512 + 512)
                    nc.vector.scalar_tensor_tensor(last[:, s, cols], bank[(4 if half == 0 else 0) + s][:],
                                                   rstd[:, 12 + s:13 + s], gains[:, 1, cols],
                                                   ALU.mult, ALU.mult).then_inc(o_scaled, 1)
                    dve.wait_ge(o_scaled, 2 * ST + 2 * s + half + 1)
                    nc.vector.tensor_tensor(last[:, s, cols], last[:, s, cols], xs[:, s, cols], ALU.add).then_inc(x_added, 1)


def rotary_table():
    inv = np.float32(10000.0) ** (-np.arange(0, HD, 2, dtype=np.float32) / np.float32(HD))
    ang = (np.arange(SEQ, dtype=np.float32)[None, :] * inv.astype(np.float32)[:, None]).astype(np.float64)
    cos = np.tile(np.cos(ang), (4, 1))
    sin = np.concatenate([-np.sin(ang), np.sin(ang)] * 2, axis=0)
    return np.stack([cos, sin], axis=1).astype(np.float32)


def decay_vectors():
    gamma = 1.0 - 2.0 ** (-5.0 - np.arange(HEADS, dtype=np.float64))
    dist = np.arange(VEC) - (P - 1)
    return np.where(dist >= 0, gamma[:, None] ** np.maximum(dist, 0), 0.0).astype(np.float32) * np.float32(HD ** -0.5)


def bucket_onehot():
    dist = np.arange(VEC) - (P - 1)
    exact = BUCKETS // 2
    far = np.maximum(dist, 1).astype(np.float64)
    large = exact + np.floor(np.log(far / exact) / math.log(MAX_DIST / exact) * (BUCKETS - exact) + 1e-9).astype(np.int64)
    bucket = np.where(dist < exact, dist, np.minimum(large, BUCKETS - 1))
    bucket = np.where(dist < 0, BUCKETS, bucket)
    return (np.arange(BUCKETS + 1)[:, None] == bucket[None, :]).astype(np.float32)


_INS = ["x", "norm_mix_pre", "w_in", "rel_bias", "w_out", "norm_mix_post", "norm_ffn_pre", "w_up",
        "conv_w", "conv_b", "w_down", "norm_ffn_post"]


def kernel(**inputs):
    import numpy as _np
    import concourse.bacc as _bacc
    from concourse import mybir as _mybir
    from concourse.bass_utils import run_bass_kernel_spmd as _run

    nc = _bacc.Bacc("TRN2", target_bir_lowering=False, num_devices=1)
    arrays, args = {}, []
    given = [(name, _np.ascontiguousarray(inputs[name])) for name in _INS]
    given += [("rotary", rotary_table()), ("decay", decay_vectors()), ("onehot", bucket_onehot())]
    for name, a in given:
        arrays[f"in_{name}_dram"] = a
        args.append(nc.dram_tensor(f"in_{name}_dram", a.shape, _mybir.dt.from_np(a.dtype), kind="ExternalInput").ap())
    args.append(nc.dram_tensor("out_0_dram", (1, SEQ, D), _mybir.dt.float32, kind="ExternalOutput").ap())
    build(nc, *args)
    r = _run(nc, [arrays], core_ids=[0])
    return r.results[0]["out_0_dram"]
```

```python
import math
from contextlib import ExitStack

import concourse.bass as bass
import numpy as np
from concourse import mybir

F32 = mybir.dt.float32
F32R = mybir.dt.float32r
ALU = mybir.AluOpType
ACT = mybir.ActivationFunctionType
AX = mybir.AxisListType

P = 128
SEQ, D = 512, 1024
HD = 64
HEADS = 8
DMIX = HEADS * HD
PAIRS = HEADS // 2
DFF = 2816
FT = DFF // P
KT = D // P
ST = SEQ // P
EPS = 1e-6
BUCKETS, MAX_DIST = 32, 128
VEC = SEQ + P
GROUPS = [1, 0, 2, 4, 3, 5, 6]
KA, QA, VA, KR, QR, VR, GR = range(7)
NU = 7
OUT0 = NU * PAIRS
UP0 = OUT0 + 2 * KT
DOWN0 = UP0 + 2 * FT
SWEEP = FT // 2
LAST_UNIT = DOWN0 + 2 * SWEEP
SLOTS = 4


def slot_of(n):
    if n < OUT0:
        return n % NU % SLOTS
    if n < DOWN0:
        return (n - OUT0) % SLOTS
    k = (n - DOWN0) % SWEEP
    return 2 if k == SWEEP - 1 else k % 2


def loads_of_slot(n):
    return sum(slot_of(m) == slot_of(n) for m in range(n + 1))


def freed_at(n):
    if n >= DOWN0:
        return n - 1
    return max((m + 1 for m in range(n) if slot_of(m) == slot_of(n)), default=0)


POOL_FROM, POOL_TO = 2, OUT0 + 2


def lo_count(n):
    if POOL_FROM <= n < POOL_TO:
        return n + 1 - POOL_FROM
    return n + 1 if n < POOL_FROM else n + 1 - (POOL_TO - POOL_FROM)


def at_turn(f, n, i, per_turn):
    if isinstance(i, int):
        return f(n + i * per_turn)
    a, b = f(n + per_turn), f(n + 2 * per_turn)
    return (b - a) * i + (2 * a - b)


def window(dram, head, rows):
    return bass.AP(dram, head * VEC, [[1, P], [VEC, rows], [1, SEQ]])


def build(nc, x, norm_mix_pre, w_in, rel_bias, w_out, norm_mix_post, norm_ffn_pre, w_up,
          conv_w, conv_b, w_down, norm_ffn_post, rotary, decay, onehot, out):
    ctx = ExitStack()
    with ctx:
        def sb(name, shape, dt=F32):
            return ctx.enter_context(nc.sbuf_tensor(name, shape, dt))

        def sem(name):
            return ctx.enter_context(nc.semaphore(name))

        xs = sb("xs", [P, ST, D])
        hT = sb("hT", [P, 2, KT, SEQ], F32R)
        yT = sb("yT", [P, 2, KT, SEQ], F32R)
        ws = sb("ws", [P, SLOTS, 2, D], F32R)
        raw = sb("raw", [P, SLOTS, D])
        gains = sb("gains", [P, 2, D])
        ident = sb("ident", [P, P])
        rot = sb("rot", [P, 2, SEQ])
        conv = sb("conv", [P, 4 * 2 * FT])
        relb = sb("relb", [BUCKETS + 1, HEADS])
        qsA = sb("qsA", [P, 2, SEQ], F32R)
        ksA = sb("ksA", [P, 2, SEQ], F32R)
        klA = sb("klA", [P, SEQ], F32R)
        qsR = sb("qsR", [P, 2, SEQ], F32R)
        ksR = sb("ksR", [P, 2, SEQ], F32R)
        klR = sb("klR", [P, SEQ], F32R)
        neghalf = sb("neghalf", [P, 8])
        sumsq = sb("sumsq", [P, 16])
        meansq = sb("meansq", [P, 16])
        rstd = sb("rstd", [P, 16])
        osum = sb("osum", [P, 2 * ST, 2])
        negmax = sb("negmax", [P, HEADS])
        rowsum = sb("rowsum", [P, HEADS])
        rowinv = sb("rowinv", [P, HEADS])
        gsum = sb("gsum", [P, HEADS])
        gneg = sb("gneg", [P, HEADS])
        gvar = sb("gvar", [P, HEADS])
        gms = sb("gms", [P, HEADS])
        grstd = sb("grstd", [P, HEADS])
        work = sb("work", [P, 11776])

        def part(at, n):
            return work[:, at:at + n]

        vA = part(0, 512)
        vArow = part(512, 512).rearrange("p (t c) -> p t c", t=ST)
        probs = part(1024, 1536).rearrange("p (r c) -> p r c", r=3)
        probsT = part(2560, 1024).rearrange("p (r c) -> p r c", r=2)
        vR = part(3584, 512)
        vRrow = part(4096, 512).rearrange("p (t c) -> p t c", t=ST)
        gate = part(4608, 512)
        rotc, rots = part(5120, 512), part(5632, 512)
        retp = part(6144, 2560).rearrange("p (h c) -> p h c", h=2)
        centered, squares = part(8704, 512), part(9216, 512)
        gated = squares
        btab = part(9728, 1024).rearrange("p (h c) -> p h c", h=2)
        dtab = part(10752, 1024).rearrange("p (h c) -> p h c", h=2)
        oneh = work[0:BUCKETS + 1, 6144:6144 + VEC]
        bvec = work[0:HEADS, 6784:6784 + VEC]
        convrows = work[0:2 * FT, 7424:7936].rearrange("t (j p) -> t j p", j=4)
        hrow = part(0, 2048).rearrange("p (r c) -> p r c", r=2)
        orow = part(2048, 2048).rearrange("p (r c) -> p r c", r=2)
        junk = part(4096, 1024)
        ojunk = part(6144, 512)
        fT = part(0, FT * SEQ).rearrange("p (t c) -> p t c", t=FT)
        ca = rot
        cb = gains[:, 0, :].rearrange("p (r c) -> p r c", r=2)
        djunk = part(FT * SEQ, 512)
        done1 = part(0, 2048).rearrange("p (s c) -> p s c", s=ST)

        def finished(s, half):
            return done1[:, s, :] if half else (ca if s < 2 else cb)[:, s % 2, :]

        bank = [ctx.enter_context(nc.psum_tensor(f"bank{b}", [P, 512], F32)) for b in range(8)]
        UNIT_BANK = [0, 1, 0, 1, 0, 1, 7]
        S_BANK, T_BANK, YA_BANK, YR_BANK = (2, 3), (4, 5), 6, 7
        O_BANK = [(0, 1), (5, 6), (2, 3), (4, 7)]
        H_BANK = [(2, 3), (4, 5), (6, 7), (2, 3)] + O_BANK
        UP_BANK = [0, 1, 5, 6]
        DOWN_BANK = [(2, 3, 4, 7), (0, 1, 5, 6)]

        x_loaded = [sem(f"x_loaded{s}") for s in range(ST)]
        raw_loaded = [sem(f"raw_loaded{s}") for s in range(SLOTS)]
        gains_loaded = sem("gains_loaded")
        gains1_loaded = sem("gains1_loaded")
        load_granted, bias_granted = sem("load_granted"), sem("bias_granted")
        gains2_loaded = sem("gains2_loaded")
        gains3_loaded = sem("gains3_loaded")
        relb_loaded, oneh_loaded = sem("relb_loaded"), sem("oneh_loaded")
        taps_loaded, cbias_loaded = sem("taps_loaded"), sem("cbias_loaded")
        rot_loaded = sem("rot_loaded")
        btab_loaded, dtab_loaded = sem("btab_loaded"), sem("dtab_loaded")
        bvec_stored = sem("bvec_stored")
        out_stored = sem("out_stored")
        const_set = sem("const_set")
        ident_set = sem("ident_set")
        conv_turned, conv_ready = sem("conv_turned"), sem("conv_ready")
        bvec_made, bvec_ready = sem("bvec_made"), sem("bvec_ready")
        sq_done, ms_done, rstd_done = sem("sq_done"), sem("ms_done"), sem("rstd_done")
        h_rows, h_turned = sem("h_rows"), sem("h_turned")
        h_hi, h_lo = sem("h_hi"), sem("h_lo")
        w_hi, w_lo, w_lo_pool, unit_done = sem("w_hi"), sem("w_lo"), sem("w_lo_pool"), sem("unit_done")

        def lo_sem(n):
            return w_lo_pool if POOL_FROM <= n < POOL_TO else w_lo

        evacuated = sem("evacuated")
        swapped, cos_done, sin_done, rotated = sem("swapped"), sem("cos_done"), sem("sin_done"), sem("rotated")
        gate_tanh, gate_sigmoid, gate_ready = sem("gate_tanh"), sem("gate_sigmoid"), sem("gate_ready")
        aq_hi, aq_lo, rq_hi, rq_lo = sem("aq_hi"), sem("aq_lo"), sem("rq_hi"), sem("rq_lo")
        vA_turned, vA_ready = sem("vA_turned"), sem("vA_ready")
        a_scores, a_biased, a_exp, a_inv = sem("a_scores"), sem("a_biased"), sem("a_exp"), sem("a_inv")
        a_probs, a_turned, a_probsT, a_pv = sem("a_probs"), sem("a_turned"), sem("a_probsT"), sem("a_pv")
        a_yhi, a_ylo = sem("a_yhi"), sem("a_ylo")
        vR_turned, vR_ready = sem("vR_turned"), sem("vR_ready")
        r_scores, r_decayed, r_pv = sem("r_scores"), sem("r_decayed"), sem("r_pv")
        r_sum, r_neg, r_centered, r_sq = sem("r_sum"), sem("r_neg"), sem("r_centered"), sem("r_sq")
        r_var, r_ms, r_rstd, r_normed = sem("r_var"), sem("r_ms"), sem("r_rstd"), sem("r_normed")
        r_turned, r_gated, r_yhi, r_ylo = sem("r_turned"), sem("r_gated"), sem("r_yhi"), sem("r_ylo")
        o_sq, o_sum, o_ms, o_rstd = sem("o_sq"), sem("o_sum"), sem("o_ms"), sem("o_rstd")
        o_scaled, x_added = sem("o_scaled"), sem("x_added")
        tap2, tap1, tap0 = sem("tap2"), sem("tap1"), sem("tap0")
        gelu_done, f_ready = sem("gelu_done"), sem("f_ready")
        f_hi, f_lo = sem("f_hi"), sem("f_lo")
        down_rows, down_gained, down_added = sem("down_rows"), sem("down_gained"), sem("down_added")
        block = ctx.enter_context(nc.Block())

        w_in_v = w_in[0].rearrange("(k p) n -> p k n", p=P)
        w_up_v = w_up[0].rearrange("(k p) n -> p k n", p=P)
        w_out_v = w_out[0].rearrange("(k p) n -> p k n", p=P)
        w_down_v = w_down[0].rearrange("(k p) n -> p k n", p=P)
        bias_dram = nc.dram_tensor("bias_vectors", (HEADS, VEC), F32, kind="Internal")

        def width(t):
            return P * (t + 1)

        def packed(mt):
            return P * mt * (mt + 1) // 2

        def f_part(c):
            return slice(512 * c, 512 * c + 512)

        @block.sync
        def _(sp):
            def load_x(s):
                sp.dma_start(xs[:, s, :], x[0, s * P:(s + 1) * P, :]).then_inc(x_loaded[s], 16)

            load_x(0)
            load_x(1)
            sp.dma_start(gains[:, 0, :], norm_mix_pre[0].partition_broadcast(P)).then_inc(gains_loaded, 16)
            load_x(2)
            load_x(3)

            def load(n, i, per_turn, source, k_major=True):
                c = slot_of(n)
                if not (isinstance(i, int) and freed_at(n + i * per_turn) == 0):
                    m = n if isinstance(i, int) else n + per_turn
                    last_unit = freed_at(m + (i * per_turn if isinstance(i, int) else 0)) - 1
                    sp.wait_ge(lo_sem(last_unit), at_turn(lambda k: lo_count(freed_at(k) - 1), n, i, per_turn))
                    if not isinstance(i, int):
                        sp.sem_inc(load_granted, 1)
                dst = raw[:, c, :]
                if k_major:
                    dst = dst.rearrange("p (k n) -> p k n", n=source.shape[-1])
                sp.dma_start(dst, source).then_inc(raw_loaded[c], 16)

            def load_turn(i, j0=0, j1=NU):
                for j in range(j0, j1):
                    load(j, i, NU, w_in_v[:, :, bass.ds(GROUPS[j] * DMIX + i * P, P)])

            load_turn(0, 0, 2)
            sp.wait_ge(const_set, 2)
            sp.dma_start(relb[0:BUCKETS, :], rel_bias).then_inc(relb_loaded, 16)
            sp.dma_start(oneh, onehot).then_inc(oneh_loaded, 16)
            sp.dma_start(convrows[:, 0:3, :], conv_w[0].rearrange("j (t p) -> t j p", p=P)).then_inc(taps_loaded, 16)
            sp.dma_start(convrows[:, 3, :], conv_b[0].rearrange("(t p) -> t p", p=P)).then_inc(cbias_loaded, 16)
            load_turn(0, 2, 4)
            sp.dma_start(rot[:], rotary).then_inc(rot_loaded, 16)
            sp.dma_start(gains[:, 1, :], norm_mix_post[0].partition_broadcast(P)).then_inc(gains1_loaded, 16)
            load_turn(0, 4, NU)
            with sp.Fori(1, PAIRS) as i:
                load_turn(i)
            for n in range(2 * KT):
                load(OUT0 + n, 0, 0, w_out_v[:, n % KT, :], k_major=False)
            with sp.Fori(0, SWEEP) as i:
                for j in range(4):
                    side, half = j % 2, j // 2
                    load(UP0 + j, i, 4, w_up_v[:, :, bass.ds(side * DFF + half * P + i * (2 * P), P)])
            for sweep in range(2):
                cols = slice(sweep * 512, sweep * 512 + 512)
                first = DOWN0 + sweep * SWEEP
                with sp.Fori(0, SWEEP // 2) as i:
                    for q in range(2):
                        load(first + q, i, 2, w_down_v[:, bass.ds(2 * q + 4 * i, 2), cols])
                load(first + SWEEP - 1, 0, 0, w_down_v[:, FT - 2:FT, cols])
            for s in range(ST):
                for half in range(2):
                    sp.wait_ge(down_added, 2 * s + half + 1)
                    sp.dma_start(out[0, s * P:(s + 1) * P, half * 512:half * 512 + 512],
                                 finished(s, half)).then_inc(out_stored, 16)
            sp.wait_ge(out_stored, 16 * 2 * ST)

        @block.gpsimd
        def _(pool):
            pool.memset(neghalf[:], -0.5).then_inc(const_set, 1)
            pool.wait_ge(const_set, 1)
            pool.memset(relb[BUCKETS:BUCKETS + 1, :], -1e30).then_inc(const_set, 1)
            pool.wait_ge(const_set, 2)
            pool.memset(ident[:], 0.0).then_inc(ident_set, 1)
            pool.wait_ge(ident_set, 1)
            pool.affine_select(out=ident[:], in_=ident[:], compare_op=ALU.not_equal, fill=1.0, base=0,
                               pattern=[[-1, P]], channel_multiplier=1).then_inc(ident_set, 1)
            pool.wait_ge(ident_set, 2)

            def row_rstd(t, src):
                nc.gpsimd.tensor_scalar(meansq[:, t:t + 1], src, 1.0 / D, EPS, ALU.mult, ALU.add).then_inc(ms_done, 1)
                pool.wait_ge(ms_done, t + 1)
                nc.gpsimd.tensor_tensor(rstd[:, t:t + 1], meansq[:, t:t + 1], neghalf[:, 0:1], ALU.pow).then_inc(rstd_done, 1)

            def out_rstd(t):
                pool.wait_ge(o_sq, 2 * t + 2 if t < ST else 2 * ST + ST + (t - ST) + 1)
                nc.gpsimd.tensor_tensor(meansq[:, 8 + t:9 + t], osum[:, t, 0:1], osum[:, t, 1:2], ALU.add).then_inc(o_sum, 1)
                pool.wait_ge(o_sum, t + 1)
                nc.gpsimd.tensor_scalar(sumsq[:, 8 + t:9 + t], meansq[:, 8 + t:9 + t], 1.0 / D, EPS,
                                        ALU.mult, ALU.add).then_inc(o_ms, 1)
                pool.wait_ge(o_ms, t + 1)
                nc.gpsimd.tensor_tensor(rstd[:, 8 + t:9 + t], sumsq[:, 8 + t:9 + t], neghalf[:, 0:1],
                                        ALU.pow).then_inc(o_rstd, 1)

            for s in range(ST):
                pool.wait_ge(sq_done, s + 1)
                row_rstd(s, sumsq[:, s:s + 1])
            pool.wait_ge(bvec_ready, 2)
            pool.dma_start(bias_dram[:, :], bvec[:]).then_inc(bvec_stored, 16)
            pool.wait_ge(bvec_stored, 16)

            def group_rstd(k):
                pool.wait_ge(r_var, k + 1)
                nc.gpsimd.tensor_scalar(gms[:], gvar[:], 1.0 / HD, EPS, ALU.mult, ALU.add).then_inc(r_ms, 1)
                pool.wait_ge(r_ms, k + 1)
                nc.gpsimd.tensor_tensor(grstd[:], gms[:], neghalf[:], ALU.pow).then_inc(r_rstd, 1)

            def split_lo(n):
                c = slot_of(n)
                pool.wait_ge(w_hi, n + 1)
                nc.gpsimd.tensor_tensor(ws[:, c, 1, :], raw[:, c, :], ws[:, c, 0, :].bitcast(F32),
                                        ALU.subtract).then_inc(w_lo_pool, 1)

            def rotary_sum(i, side):
                pool.wait_ge(sin_done, 2 * i + side + 1)
                nc.gpsimd.tensor_tensor(rotc, rotc, rots, ALU.add).then_inc(rotated, 1)

            for i in range(PAIRS):
                if i:
                    pool.wait_ge(a_biased, 8 * i)
                pool.dma_start(btab, window(bias_dram, 2 * i, 2)).then_inc(btab_loaded, 16)
                split_lo(NU * i + 2)
                split_lo(NU * i + 3)
                split_lo(NU * i + 4)
                if i:
                    pool.wait_ge(r_decayed, 8 * i)
                pool.dma_start(dtab, window(decay.tensor, 2 * i, 2)).then_inc(dtab_loaded, 16)
                split_lo(NU * i + 5)
                if i:
                    group_rstd(i - 1)
                split_lo(NU * i + 6)
                rotary_sum(i, 0)
                split_lo(NU * i + 7)
                rotary_sum(i, 1)
                split_lo(NU * i + 8)
            group_rstd(PAIRS - 1)
            pool.wait_ge(h_rows, ST)
            pool.dma_start(gains[:, 0, :], norm_ffn_pre[0].partition_broadcast(P)).then_inc(gains2_loaded, 16)
            for pair in ((0, 1), (2, 3)):
                for s in pair:
                    out_rstd(s)
                for s in pair:
                    pool.wait_ge(sq_done, ST + s + 1)
                    row_rstd(ST + s, sumsq[:, ST + s:ST + s + 1])
            pool.wait_ge(o_scaled, 2 * ST)
            pool.dma_start(gains[:, 1, :], norm_ffn_post[0].partition_broadcast(P)).then_inc(gains3_loaded, 16)
            for s in range(ST):
                out_rstd(ST + s)

        @block.tensor
        def _(pe):
            def three(dst, st_hi, st_lo, mv_hi, mv_lo, p, start, stop):
                st, mv = ((st_hi, mv_hi), (st_hi, mv_lo), (st_lo, mv_hi))[p]
                return nc.tensor.matmul(dst, st, mv, start=start, stop=stop)

            def turn_rows(t):
                banks = H_BANK[t]
                pe.wait_ge(h_rows, t + 1)
                for half in range(2):
                    if t == 3:
                        pe.wait_ge(h_lo, 2)
                    for k in range(4):
                        c = (4 * half + k) * P
                        ins = nc.tensor.transpose(bank[banks[half]][:, k * P:(k + 1) * P],
                                                  hrow[:, t % 2, c:c + P], ident[:])
                    ins.then_inc(h_turned, 1)

            def column_unit(n, dst, m0, m1, part=slice(0, SEQ), finish=True):
                c = slot_of(n)
                for m in range(m0, m1):
                    k, p = divmod(m, 3)
                    cols = slice(k * P, (k + 1) * P)
                    ins = three(dst[:, part], ws[:, c, 0, cols], ws[:, c, 1, cols], hT[:, 0, k, part], hT[:, 1, k, part],
                                p, m == 0, m == 23)
                if m1 == 24 and finish:
                    ins.then_inc(unit_done, 1)

            FRONT, BACK = slice(0, SEQ // 2), slice(SEQ // 2, SEQ)

            def project(i, j, m0, m1):
                if m0 == 0:
                    pe.wait_ge(w_lo_pool, at_turn(lo_count, j, i, NU))
                    first = isinstance(i, int) and i == 0
                    if j == 0 and not first:
                        pe.wait_ge(cos_done, 2 * i)
                    if j == 1 and not first:
                        pe.wait_ge(evacuated, 2 * i)
                    if j in (2, 3):
                        pe.wait_ge(aq_lo, 2 * i + (j - 1))
                    if j == 4:
                        pe.wait_ge(evacuated, 2 * i + 1)
                    if j == 5:
                        pe.wait_ge(cos_done, 2 * i + 1)
                    if j == 6 and not first:
                        pe.wait_ge(r_gated, i * 1)
                column_unit(j, bank[UNIT_BANK[j]], m0, m1)

            def ret_values(k):
                pe.wait_ge(evacuated, 2 * k + 2)
                pe.wait_ge(a_probsT, 8 * k + 8)
                for t in range(ST):
                    ins = nc.tensor.transpose(bank[T_BANK[0]][:, t * P:(t + 1) * P], vR[:, t * P:(t + 1) * P], ident[:])
                ins.then_inc(vR_turned, 1)

            def ret_scores(k, u):
                h, mt = u // 4, 3 - u % 4
                if u == 0:
                    pe.wait_ge(rq_lo, 2 * k + 2)
                    pe.wait_ge(a_biased, 8 * k + 8)
                if u >= 2:
                    pe.wait_ge(r_decayed, 8 * k + u - 1)
                rows = slice(HD * h, HD * h + HD)
                dst, tile, wide = bank[S_BANK[u % 2]][:, 0:width(mt)], slice(mt * P, (mt + 1) * P), slice(SEQ - width(mt), SEQ)
                nc.tensor.matmul(dst, ksR[:, h, tile], qsR[:, h, wide], start=True, stop=False)
                nc.tensor.matmul(dst, klR[rows, tile], qsR[rows, h, wide], start=False, stop=True).then_inc(r_scores, 1)

            def ret_mix(k, u):
                h, nt = u // 4, u % 4
                if u == 0:
                    pe.wait_ge(vR_ready, 1 * k + 1)
                    pe.wait_ge(gate_ready, 1 * k + 1)
                pe.wait_ge(r_decayed, 8 * k + u + 1)
                for mt in range(3 - nt, 4):
                    c = packed(mt) + nt * P - (SEQ - width(mt))
                    ins = nc.tensor.matmul(bank[YR_BANK][:, (2 * nt + h) * HD:(2 * nt + h + 1) * HD],
                                           retp[:, h, c:c + P], vRrow[:, mt, HD * h:HD * h + HD],
                                           start=mt == 3 - nt, stop=mt == 3)
                if u == 7:
                    ins.then_inc(r_pv, 1)

            def ret_turn_out(k):
                pe.wait_ge(r_normed, 1 * k + 1)
                for t in range(ST):
                    ins = nc.tensor.transpose(bank[YR_BANK][:, t * P:(t + 1) * P],
                                              centered[:, t * P:(t + 1) * P], ident[:])
                ins.then_inc(r_turned, 1)

            def moba_values(i):
                pe.wait_ge(evacuated, 2 * i + 1)
                for t in range(ST):
                    ins = nc.tensor.transpose(bank[T_BANK[1]][:, t * P:(t + 1) * P], vA[:, t * P:(t + 1) * P], ident[:])
                ins.then_inc(vA_turned, 1)

            def moba_scores(i, u, first):
                h, qt = u // 4, u % 4
                if u == 0:
                    pe.wait_ge(aq_lo, 2 * i + 2)
                if u < 2 and not first:
                    pe.wait_ge(r_decayed, 8 * i)
                if u >= 2:
                    pe.wait_ge(a_biased, 8 * i + u - 1)
                rows = slice(HD * h, HD * h + HD)
                dst, tile, wide = bank[S_BANK[u % 2]][:, 0:width(qt)], slice(qt * P, (qt + 1) * P), slice(SEQ - width(qt), SEQ)
                nc.tensor.matmul(dst, qsA[:, h, tile], ksA[:, h, wide], start=True, stop=False)
                nc.tensor.matmul(dst, qsA[rows, h, tile], klA[rows, wide], start=False, stop=True).then_inc(a_scores, 1)

            def moba_turn(i, u):
                qt = u % 4
                pe.wait_ge(a_probs, 8 * i + u + 1)
                if u < 2:
                    pe.wait_ge(vA_ready, 1 * i + 1)
                else:
                    pe.wait_ge(a_probsT, 8 * i + u - 1)
                for t in range(qt + 1):
                    ins = nc.tensor.transpose(bank[T_BANK[u % 2]][:, t * P:(t + 1) * P],
                                              probs[:, u % 3, t * P:(t + 1) * P], ident[:])
                ins.then_inc(a_turned, 1)

            def moba_mix(i, u, first):
                h, qt = u // 4, u % 4
                if u == 0 and not first:
                    pe.wait_ge(a_ylo, 1 * i)
                pe.wait_ge(a_probsT, 8 * i + u + 1)
                for t in range(qt + 1):
                    ins = nc.tensor.matmul(bank[YA_BANK][HD * h:HD * h + HD, qt * P:(qt + 1) * P],
                                           vArow[:, 3 - qt + t, HD * h:HD * h + HD],
                                           probsT[:, u % 2, t * P:(t + 1) * P], start=t == 0, stop=t == qt)
                ins.then_inc(a_pv, 1)

            def mixer_turn(i, first):
                for r in range(6 if first else 0, 9):
                    project(i, r // 3, 8 * (r % 3), 8 * (r % 3) + 8)
                    if not first:
                        if r == 0:
                            ret_values(i - 1)
                        if r >= 2:
                            ret_mix(i - 1, r - 2)
                        if r < 8:
                            ret_scores(i - 1, r)
                for u in range(12):
                    project(i, 3 + u // 3, 8 * (u % 3), 8 * (u % 3) + 8)
                    if u == 0:
                        if not first:
                            ret_mix(i - 1, 7)
                        moba_values(i)
                    if u == 5 and not first:
                        ret_turn_out(i - 1)
                    if 3 <= u < 11:
                        moba_mix(i, u - 3, first)
                    if u < 8:
                        moba_scores(i, u, first)
                    if 2 <= u < 10:
                        moba_turn(i, u - 2)

            pe.wait_ge(ident_set, 2)
            turn_rows(0)
            turn_rows(1)
            pe.wait_ge(h_lo, 4)
            pe.wait_ge(w_lo, 1)
            column_unit(0, bank[0], 0, 24, FRONT, False)
            turn_rows(2)
            pe.wait_ge(w_lo, 2)
            column_unit(1, bank[1], 0, 24, FRONT, False)
            turn_rows(3)
            pe.wait_ge(taps_loaded, 16)
            pe.wait_ge(cbias_loaded, 16)
            for j in range(4):
                ins = nc.tensor.transpose(bank[4][:, j * 2 * FT:(j + 1) * 2 * FT], convrows[:, j, :],
                                          ident[0:2 * FT, 0:2 * FT])
            ins.then_inc(conv_turned, 1)
            pe.wait_ge(relb_loaded, 16)
            pe.wait_ge(oneh_loaded, 16)
            pe.wait_ge(const_set, 2)
            pe.wait_ge(h_lo, 6)
            for b, lo, hi in ((5, 0, 512), (6, 512, VEC)):
                ins = nc.tensor.matmul(bank[b][0:HEADS, 0:hi - lo], relb[:], oneh[:, lo:hi], start=True, stop=True)
            ins.then_inc(bvec_made, 1)
            pe.wait_ge(h_lo, 2 * ST)
            column_unit(0, bank[0], 0, 24, BACK)
            column_unit(1, bank[1], 0, 24, BACK)
            pe.wait_ge(bvec_ready, 2)
            pe.wait_ge(conv_ready, 1)
            mixer_turn(0, True)
            with pe.Fori(1, PAIRS) as i:
                mixer_turn(i, False)

            def out_rows(pass_, m0, m1):
                for m in range(m0, m1):
                    k, r = divmod(m, 12)
                    n = OUT0 + pass_ * KT + k
                    s, half, p = 2 * pass_ + r // 6, r // 3 % 2, r % 3
                    if r == 0:
                        pe.wait_ge(lo_sem(n), lo_count(n))
                        if pass_ == 0 and k < PAIRS:
                            pe.wait_ge(a_ylo, k + 1)
                        if pass_ == 0 and k >= PAIRS:
                            pe.wait_ge(r_ylo, k - PAIRS + 1)
                    rows = slice(s * P, (s + 1) * P)
                    c = slot_of(n)
                    ins = three(bank[O_BANK[s][half]][:], yT[:, 0, k, rows], yT[:, 1, k, rows],
                                ws[:, c, 0, half * 512:half * 512 + 512], ws[:, c, 1, half * 512:half * 512 + 512],
                                p, k == 0 and p == 0, k == KT - 1 and p == 2)
                    if r == 11:
                        ins.then_inc(unit_done, 1)

            k = PAIRS - 1
            pe.wait_ge(cos_done, 2 * PAIRS)
            pe.wait_ge(evacuated, 2 * PAIRS)
            for r in range(10):
                if r == 0:
                    ret_values(k)
                if r >= 2:
                    ret_mix(k, r - 2)
                if r < 8:
                    ret_scores(k, r)
                if r == 0:
                    pe.wait_ge(a_ylo, PAIRS)
                out_rows(0, 5 * r, 5 * r + 5)
            out_rows(0, 50, 84)
            ret_turn_out(k)
            out_rows(0, 84, 96)
            pe.wait_ge(r_gated, PAIRS)
            pe.wait_ge(r_decayed, 8 * PAIRS)
            pe.wait_ge(vR_ready, PAIRS)
            for k in range(KT):
                out_rows(1, 12 * k, 12 * k + 12)
                if k == 4:
                    turn_rows(ST)
                if k == 6:
                    turn_rows(ST + 1)

            for j in range(4):
                if j == 0:
                    pe.wait_ge(h_lo, 2 * ST + 4)
                if j == 3:
                    turn_rows(ST + 2)
                pe.wait_ge(w_lo, lo_count(UP0 + j))
                column_unit(UP0 + j, bank[UP_BANK[j]], 0, 24, FRONT, False)
            turn_rows(ST + 3)
            pe.wait_ge(h_lo, 4 * ST)
            for j in range(4):
                column_unit(UP0 + j, bank[UP_BANK[j]], 0, 24, BACK)
            with pe.Fori(1, SWEEP) as i:
                for j in range(4):
                    pe.wait_ge(w_lo, 4 * i + lo_count(UP0 + j))
                    pe.wait_ge(tap0, 4 * i + (j - 3))
                    column_unit(UP0 + j, bank[UP_BANK[j]], 0, 24)

            def down_product(sweep, c, kk, s, start, stop):
                cols, rows = slice(kk * 512, kk * 512 + 512), slice(s * P, (s + 1) * P)
                for p in range(3):
                    ins = three(bank[DOWN_BANK[sweep][s]][:], yT[:, 0, 2 * c + kk, rows], yT[:, 1, 2 * c + kk, rows],
                                ws[:, c, 0, cols], ws[:, c, 1, cols], p, start and p == 0, stop and p == 2)
                return ins

            def down_unit(sweep, n0, q, i, start):
                pe.wait_ge(w_lo, 2 * i + lo_count(n0 + q))
                pe.wait_ge(f_lo, 4 * i + (2 * (n0 - DOWN0 + q) + 2))
                for kk in range(2):
                    for s in range(ST):
                        ins = down_product(sweep, slot_of(n0 + q), kk, s, start and kk == 0, False)
                ins.then_inc(unit_done, 1)

            for sweep in range(2):
                first = DOWN0 + sweep * SWEEP
                if sweep == 0:
                    pe.wait_ge(h_lo, 4 * ST)
                else:
                    pe.wait_ge(tap0, 2 * 2 * FT // 2)
                for q in range(2):
                    down_unit(sweep, first, q, 0, q == 0)
                with pe.Fori(1, SWEEP // 2) as i:
                    for q in range(2):
                        down_unit(sweep, first, q, i, False)
                n = first + SWEEP - 1
                pe.wait_ge(w_lo, lo_count(n))
                pe.wait_ge(f_lo, 2 * (n - DOWN0) + 2)
                for s in range(ST):
                    down_product(sweep, slot_of(n), 0, s, False, False)
                    down_product(sweep, slot_of(n), 1, s, False, True).then_inc(down_rows, 1)
                pe.wait_ge(down_rows, ST * sweep + ST)
                pe.sem_inc(unit_done, 1)

        @block.scalar
        def _(act):
            def split_hi(n, i=0, per_turn=0):
                c = slot_of(n)
                act.wait_ge(raw_loaded[c], at_turn(lambda m: 16 * loads_of_slot(m), n, i, per_turn)
                            if n < DOWN0 else 16 * (i * 1) + 16 * loads_of_slot(n))
                if not (isinstance(i, int) and freed_at(n + i * per_turn) == 0):
                    act.wait_ge(unit_done, at_turn(freed_at, n, i, per_turn))
                nc.scalar.activation(ws[:, c, 0, :], raw[:, c, :], ACT.Copy).then_inc(w_hi, 1)

            def h_evacuate(t):
                banks = H_BANK[t]
                s = t % ST
                for half in range(2):
                    act.wait_ge(h_turned, 2 * t + half + 1)
                    nc.scalar.activation(hT[:, 0, 4 * half:4 * half + 4, s * P:(s + 1) * P],
                                         bank[banks[half]][:].rearrange("p (k c) -> p k c", k=4),
                                         ACT.Copy).then_inc(h_hi, 1)

            def row_squares(t):
                if t:
                    act.wait_ge(sq_done, t)
                nc.scalar.activation(junk, xs[:, t % ST, :], ACT.Square, accum_out=sumsq[:, t:t + 1]).then_inc(sq_done, 1)

            for s in range(2):
                act.wait_ge(x_loaded[s], 16)
                row_squares(s)
            h_evacuate(0)
            act.wait_ge(x_loaded[2], 16)
            row_squares(2)
            split_hi(0)
            h_evacuate(1)
            act.wait_ge(x_loaded[3], 16)
            row_squares(3)
            split_hi(1)
            h_evacuate(2)
            h_evacuate(3)
            act.wait_ge(conv_turned, 1)
            nc.scalar.activation(conv[:], bank[4][:, 0:8 * FT], ACT.Copy).then_inc(conv_ready, 1)
            act.wait_ge(bvec_made, 1)
            for b, lo, hi in ((5, 0, 512), (6, 512, VEC)):
                nc.scalar.activation(bvec[:, lo:hi], bank[b][0:HEADS, 0:hi - lo], ACT.Copy, scale=8.0).then_inc(bvec_ready, 1)

            def stack_hi(src, keys, queries, side, signal):
                for h in range(2):
                    own, other = slice(HD * h, HD * h + HD), slice(HD * (1 - h), HD * (1 - h) + HD)
                    if side == 0:
                        nc.scalar.activation(keys[own, h, ::-1], src[own, :], ACT.Copy)
                        ins = nc.scalar.activation(keys[other, h, ::-1], src[own, :], ACT.Copy)
                    else:
                        ins = nc.scalar.activation(queries[own, h, :], src[own, :], ACT.Copy)
                ins.then_inc(signal, 1)

            def evacuate(i, j, dst, first):
                act.wait_ge(unit_done, at_turn(lambda n: n + 1, j, i, NU))
                nc.scalar.activation(dst, bank[UNIT_BANK[j]][:], ACT.Copy).then_inc(evacuated, 1)

            def swap_halves(i, j, first):
                act.wait_ge(unit_done, at_turn(lambda n: n + 1, j, i, NU))
                if j == QR or not first:
                    act.wait_ge(rotated, 2 * i + (j - KR))
                for b in range(4):
                    src = 32 * (b ^ 1)
                    ins = nc.scalar.activation(rots[32 * b:32 * b + 32, :], bank[UNIT_BANK[j]][src:src + 32, :], ACT.Copy)
                ins.then_inc(swapped, 1)

            def gate_halftanh(k):
                act.wait_ge(unit_done, at_turn(lambda n: n + 1, GR, k, NU))
                nc.scalar.activation(gate, bank[UNIT_BANK[GR]][:], ACT.Tanh, scale=0.5).then_inc(gate_tanh, 1)

            def moba_stack(i, side, first):
                act.wait_ge(unit_done, at_turn(lambda n: n + 1, KA + side, i, NU))
                if not first:
                    act.wait_ge(a_scores, 8 * i)
                stack_hi(bank[UNIT_BANK[KA + side]], ksA, qsA, side, aq_hi)

            def ret_stack(i, side, first):
                act.wait_ge(rotated, 2 * i + side + 1)
                if not first:
                    act.wait_ge(r_scores, 8 * i)
                stack_hi(rotc, ksR, qsR, side, rq_hi)

            def mixer_turn(i, first):
                for r in range(9):
                    if r == 0 and not first:
                        gate_halftanh(i - 1)
                        act.wait_ge(vR_turned, 1 * i)
                        nc.scalar.activation(vRrow, bank[T_BANK[0]][:].rearrange("p (t c) -> p t c", t=ST),
                                             ACT.Copy).then_inc(vR_ready, 1)
                    if r == 3:
                        moba_stack(i, 0, first)
                    if r == 6:
                        moba_stack(i, 1, first)
                    if r % 3 == 1:
                        split_hi(r // 3 + 2, i, NU)
                for u in range(12):
                    if u == 0:
                        evacuate(i, VA, vA[:, ::-1], first)
                    if u == 3:
                        swap_halves(i, KR, first)
                    if u == 6:
                        swap_halves(i, QR, first)
                    if u == 9:
                        evacuate(i, VR, vR[:, ::-1], first)
                    if u == 1:
                        if not first:
                            act.wait_ge(a_pv, 8 * i)
                        act.wait_ge(vA_turned, 1 * i + 1)
                        nc.scalar.activation(vArow, bank[T_BANK[1]][:].rearrange("p (t c) -> p t c", t=ST),
                                             ACT.Copy).then_inc(vA_ready, 1)
                    if u == 2 and not first:
                        act.wait_ge(r_centered, 1 * i)
                        nc.scalar.activation(squares, centered, ACT.Square).then_inc(r_sq, 1)
                    if 2 <= u < 10:
                        v = u - 2
                        w = width(v % 4)
                        act.wait_ge(a_turned, 8 * i + v + 1)
                        if v >= 2:
                            act.wait_ge(a_pv, 8 * i + v - 1)
                        nc.scalar.activation(probsT[:, v % 2, 0:w], bank[T_BANK[v % 2]][:, 0:w],
                                             ACT.Copy).then_inc(a_probsT, 1)
                    if u < 8:
                        w = width(u % 4)
                        act.wait_ge(a_biased, 8 * i + u + 1)
                        nc.scalar.activation(probs[:, u % 3, 0:w], probs[:, u % 3, 0:w], ACT.Exp, scale=-1.0,
                                             bias=negmax[:, u:u + 1], accum_out=rowsum[:, u:u + 1]).then_inc(a_exp, 1)
                    if u == 6 and not first:
                        act.wait_ge(r_gated, 1 * i)
                        nc.scalar.activation(yT[:, 0, i + (PAIRS - 1), :] if isinstance(i, int)
                                             else yT[:, 0, bass.ds(i + (PAIRS - 1), 1), :].rearrange("p o c -> p (o c)"),
                                             gated, ACT.Copy).then_inc(r_yhi, 1)
                    if u == 5:
                        ret_stack(i, 0, first)
                    if u == 8:
                        ret_stack(i, 1, first)
                    if u % 3 == 1:
                        split_hi(u // 3 + 5, i, NU)
                act.wait_ge(a_pv, 8 * i + 8)
                nc.scalar.activation(yT[:, 0, i, :] if isinstance(i, int)
                                     else yT[:, 0, bass.ds(i, 1), :].rearrange("p o c -> p (o c)"),
                                     bank[YA_BANK][:], ACT.Copy).then_inc(a_yhi, 1)

            mixer_turn(0, True)
            with act.Fori(1, PAIRS) as i:
                mixer_turn(i, False)

            k = PAIRS - 1
            gate_halftanh(k)
            act.wait_ge(vR_turned, PAIRS)
            nc.scalar.activation(vRrow, bank[T_BANK[0]][:].rearrange("p (t c) -> p t c", t=ST), ACT.Copy).then_inc(vR_ready, 1)
            for n in range(2, 7):
                split_hi(OUT0 + n)
            act.wait_ge(r_centered, PAIRS)
            nc.scalar.activation(squares, centered, ACT.Square).then_inc(r_sq, 1)
            split_hi(OUT0 + 7)
            split_hi(OUT0 + 8)
            act.wait_ge(r_gated, PAIRS)
            nc.scalar.activation(yT[:, 0, KT - 1, :], gated, ACT.Copy).then_inc(r_yhi, 1)
            split_hi(OUT0 + 9)

            def out_squares(s):
                for half in range(2):
                    if s or half:
                        act.wait_ge(o_sq, 2 * s + half)
                    nc.scalar.activation(ojunk, bank[O_BANK[s][half]][:], ACT.Square,
                                         accum_out=osum[:, s, half:half + 1]).then_inc(o_sq, 1)

            def x_squares(s):
                act.wait_ge(x_added, s + 1)
                row_squares(ST + s)

            for k in range(KT):
                if k == 0:
                    act.wait_ge(unit_done, OUT0 + KT)
                    out_squares(0)
                    out_squares(1)
                if k == 2:
                    x_squares(0)
                if k == 3:
                    x_squares(1)
                if k == 5:
                    h_evacuate(ST)
                if k == 7:
                    h_evacuate(ST + 1)
                split_hi(OUT0 + KT + k + 2)
            act.wait_ge(unit_done, UP0)
            out_squares(2)
            out_squares(3)
            split_hi(UP0 + 2)
            split_hi(UP0 + 3)
            for s in (2, 3):
                x_squares(s)
            for s in (2, 3):
                h_evacuate(ST + s)

            def up_post(i, j, first):
                t = 2 * i + ((FT if j % 2 else 0) + j // 2)
                dst = (cb if j % 2 else ca)[:, j // 2, :]
                act.wait_ge(unit_done, 4 * i + (UP0 + j + 1))
                if not first:
                    act.wait_ge(f_ready, 2 * i + (j // 2 - 1))
                def col(tap):
                    c = 2 * FT * tap + t
                    return conv[:, c:c + 1] if isinstance(c, int) else conv[:, bass.ds(c, 1)]
                nc.scalar.activation(dst, bank[UP_BANK[j]][:], ACT.Identity, scale=col(2), bias=col(3)).then_inc(tap2, 1)
                if j % 2:
                    act.wait_ge(tap0, 4 * i + j)
                    nc.scalar.activation(ca[:, j // 2, :], ca[:, j // 2, :], ACT.Gelu_apprx_tanh).then_inc(gelu_done, 1)

            def f_split_hi(n0, q, i):
                for kk in range(2):
                    k0 = 2 * ((n0 - DOWN0) % SWEEP + q) + kk
                    k = 4 * i + k0
                    src = fT[:, k, :] if isinstance(k, int) else fT[:, bass.ds(k, 1), :].rearrange("p o c -> p (o c)")
                    nc.scalar.activation(yT[:, 0, 2 * slot_of(n0 + q) + kk, :], src, ACT.Copy).then_inc(f_hi, 1)

            def down_squares(sweep):
                for s in range(ST):
                    act.wait_ge(down_rows, ST * sweep + s + 1)
                    act.wait_ge(o_sq, 2 * ST + ST * sweep + s)
                    nc.scalar.activation(djunk, bank[DOWN_BANK[sweep][s]][:], ACT.Square,
                                         accum_out=osum[:, ST + s, sweep:sweep + 1]).then_inc(o_sq, 1)

            def down_hi(n0, q, i):
                c = slot_of(n0 + q)
                act.wait_ge(raw_loaded[c], 16 * i + 16 * loads_of_slot(n0 + q))
                act.wait_ge(unit_done, 2 * i + (n0 + q - 1))
                nc.scalar.activation(ws[:, c, 0, :], raw[:, c, :], ACT.Copy).then_inc(w_hi, 1)
                f_split_hi(n0, q, i)

            for j in range(4):
                if j >= 2:
                    split_hi(UP0 + 2 + j)
                up_post(0, j, True)
            with act.Fori(1, SWEEP - 1) as i:
                for j in range(4):
                    split_hi(UP0 + 2 + j, i, 4)
                    up_post(i, j, False)
            for j in range(4):
                if j < 2:
                    split_hi(UP0 + 2 + j, SWEEP - 1, 4)
                else:
                    down_hi(DOWN0, j - 2, 0)
                up_post(SWEEP - 1, j, False)
            for sweep in range(2):
                first = DOWN0 + sweep * SWEEP
                if sweep:
                    for q in range(2):
                        down_hi(first, q, 0)
                    down_squares(0)
                with act.Fori(1, SWEEP // 2) as i:
                    for q in range(2):
                        down_hi(first, q, i)
                if sweep == 0:
                    act.wait_ge(f_ready, FT)
                down_hi(first + SWEEP - 1, 0, 0)
            down_squares(1)

        @block.vector
        def _(dve):
            def f32(ap):
                return ap.bitcast(F32)

            def split_lo(n, i=0, per_turn=0):
                c = slot_of(n)
                dve.wait_ge(w_hi, at_turn(lambda m: m + 1, n, i, per_turn))
                nc.vector.tensor_tensor(ws[:, c, 1, :], raw[:, c, :], f32(ws[:, c, 0, :]), ALU.subtract).then_inc(w_lo, 1)

            def normed_rows(t):
                dve.wait_ge(rstd_done, t + 1)
                if t >= 2:
                    dve.wait_ge(h_turned, 2 * (t - 1))
                nc.vector.scalar_tensor_tensor(hrow[:, t % 2, :], xs[:, t % ST, :], rstd[:, t:t + 1],
                                               gains[:, 0, :], ALU.mult, ALU.mult).then_inc(h_rows, 1)

            def h_low(t):
                banks = H_BANK[t]
                s = t % ST
                for half in range(2):
                    dve.wait_ge(h_hi, 2 * t + half + 1)
                    cols = (slice(None), slice(4 * half, 4 * half + 4), slice(s * P, (s + 1) * P))
                    nc.vector.tensor_tensor(hT[:, 1, 4 * half:4 * half + 4, s * P:(s + 1) * P],
                                            bank[banks[half]][:].rearrange("p (k c) -> p k c", k=4),
                                            f32(hT[:, 0, 4 * half:4 * half + 4, s * P:(s + 1) * P]),
                                            ALU.subtract).then_inc(h_lo, 1)

            dve.wait_ge(gains_loaded, 16)
            normed_rows(0)
            normed_rows(1)
            h_low(0)
            normed_rows(2)
            h_low(1)
            split_lo(0)
            normed_rows(3)
            split_lo(1)
            h_low(2)
            h_low(3)
            dve.wait_ge(rot_loaded, 16)

            def gate_finish(k):
                dve.wait_ge(gate_tanh, 1 * k + 1)
                nc.vector.tensor_scalar(gate, gate, 0.5, 0.5, ALU.mult, ALU.add).then_inc(gate_sigmoid, 1)
                dve.wait_ge(gate_sigmoid, 1 * k + 1)
                nc.vector.tensor_tensor(gate, bank[UNIT_BANK[GR]][:], gate, ALU.mult).then_inc(gate_ready, 1)

            def stack_lo(src, keys, keys_lo, queries, side, signal):
                for h in range(2):
                    own, other = slice(HD * h, HD * h + HD), slice(HD * (1 - h), HD * (1 - h) + HD)
                    if side == 0:
                        ins = nc.vector.tensor_tensor(keys_lo[own, ::-1], src[own, :], f32(keys[own, h, ::-1]), ALU.subtract)
                    else:
                        ins = nc.vector.tensor_tensor(queries[other, h, :], src[own, :], f32(queries[own, h, :]), ALU.subtract)
                ins.then_inc(signal, 1)

            def moba_stack(i, side):
                dve.wait_ge(aq_hi, 2 * i + side + 1)
                stack_lo(bank[UNIT_BANK[KA + side]], ksA, klA, qsA, side, aq_lo)

            def ret_stack(i, side):
                dve.wait_ge(rq_hi, 2 * i + side + 1)
                stack_lo(rotc, ksR, klR, qsR, side, rq_lo)

            def ret_decay(k, u):
                h, mt = u // 4, 3 - u % 4
                if u == 0:
                    dve.wait_ge(dtab_loaded, 16 * k + 16)
                dve.wait_ge(r_scores, 8 * k + u + 1)
                nc.vector.tensor_tensor(retp[:, h, packed(mt):packed(mt) + width(mt)],
                                        bank[S_BANK[u % 2]][:, 0:width(mt)], dtab[:, h, 0:width(mt)],
                                        ALU.mult).then_inc(r_decayed, 1)

            def grouped(ap):
                return ap.rearrange("p (g e) -> p g e", e=HD)

            def spread(ap):
                return ap.unsqueeze(2).to_broadcast([P, HEADS, HD])

            def ret_center(k):
                dve.wait_ge(r_pv, 1 * k + 1)
                nc.vector.tensor_reduce(gsum[:], grouped(bank[YR_BANK][:]), AX.X, ALU.add).then_inc(r_sum, 1)
                dve.wait_ge(r_sum, 1 * k + 1)
                nc.vector.tensor_scalar(gneg[:], gsum[:], -1.0 / HD, None, ALU.mult).then_inc(r_neg, 1)
                dve.wait_ge(r_neg, 1 * k + 1)
                nc.vector.tensor_tensor(grouped(centered), grouped(bank[YR_BANK][:]), spread(gneg[:]),
                                        ALU.add).then_inc(r_centered, 1)

            def ret_variance(k):
                dve.wait_ge(r_sq, 1 * k + 1)
                nc.vector.tensor_reduce(gvar[:], grouped(squares), AX.X, ALU.add).then_inc(r_var, 1)

            def ret_norm(k):
                dve.wait_ge(r_rstd, 1 * k + 1)
                nc.vector.tensor_tensor(grouped(centered), grouped(centered), spread(grstd[:]),
                                        ALU.mult).then_inc(r_normed, 1)

            def ret_gate(k):
                dve.wait_ge(r_turned, 1 * k + 1)
                nc.vector.tensor_tensor(gated, bank[YR_BANK][:], gate, ALU.mult).then_inc(r_gated, 1)

            def y_slice(half, k):
                return (yT[:, half, k, :] if isinstance(k, int)
                        else yT[:, half, bass.ds(k, 1), :].rearrange("p o c -> p (o c)"))

            def ret_low(k):
                dve.wait_ge(r_yhi, 1 * k + 1)
                nc.vector.tensor_tensor(y_slice(1, k + PAIRS), gated, f32(y_slice(0, k + PAIRS)),
                                        ALU.subtract).then_inc(r_ylo, 1)

            def bias_and_max(i, u, first):
                h, w = u // 4, width(u % 4)
                if u == 0:
                    dve.wait_ge(btab_loaded, 16 * i + 16)
                dve.wait_ge(a_scores, 8 * i + u + 1)
                if u >= 3:
                    dve.wait_ge(a_turned, 8 * i + u - 2)
                if not first:
                    dve.sem_inc(bias_granted, 1)
                nc.vector.tensor_tensor_reduce(out=probs[:, u % 3, 0:w], in0=bank[S_BANK[u % 2]][:, 0:w],
                                               in1=btab[:, h, 0:w], scale=-0.125, scalar=3.0e38, op0=ALU.add,
                                               op1=ALU.min, accum_out=negmax[:, u:u + 1]).then_inc(a_biased, 1)

            def normalise(i, u):
                w = width(u % 4)
                dve.wait_ge(a_exp, 8 * i + u + 1)
                nc.vector.reciprocal(rowinv[:, u:u + 1], rowsum[:, u:u + 1]).then_inc(a_inv, 1)
                dve.wait_ge(a_inv, 8 * i + u + 1)
                nc.vector.tensor_scalar(probs[:, u % 3, 0:w], probs[:, u % 3, 0:w], rowinv[:, u:u + 1], None,
                                        ALU.mult).then_inc(a_probs, 1)

            def rotate(i, j):
                side = j - KR
                dve.wait_ge(swapped, 2 * i + side + 1)
                nc.vector.tensor_tensor(rotc, bank[UNIT_BANK[j]][:], rot[:, 0, :], ALU.mult).then_inc(cos_done, 1)
                nc.vector.tensor_tensor(rots, rots, rot[:, 1, :], ALU.mult).then_inc(sin_done, 1)

            def mixer_turn(i, first):
                for r in range(9):
                    if r == 0 and not first:
                        gate_finish(i - 1)
                    if r < 8 and not first:
                        ret_decay(i - 1, r)
                    if r == 3:
                        moba_stack(i, 0)
                    if r == 6:
                        moba_stack(i, 1)
                for u in range(12):
                    if 1 <= u < 9:
                        normalise(i, u - 1)
                    if u < 8:
                        bias_and_max(i, u, first)
                    if not first:
                        if u == 1:
                            ret_center(i - 1)
                        if u == 3:
                            ret_variance(i - 1)
                        if u == 4:
                            ret_norm(i - 1)
                        if u == 6:
                            ret_gate(i - 1)
                        if u == 7:
                            ret_low(i - 1)
                    if u == 4:
                        rotate(i, KR)
                    if u == 6:
                        ret_stack(i, 0)
                    if u == 7:
                        rotate(i, QR)
                    if u == 9:
                        ret_stack(i, 1)
                dve.wait_ge(a_yhi, 1 * i + 1)
                nc.vector.tensor_tensor(y_slice(1, i), bank[YA_BANK][:], f32(y_slice(0, i)), ALU.subtract).then_inc(a_ylo, 1)

            mixer_turn(0, True)
            with dve.Fori(1, PAIRS) as i:
                mixer_turn(i, False)

            k = PAIRS - 1
            gate_finish(k)
            for r in range(8):
                ret_decay(k, r)
                if r in (1, 3, 5, 6):
                    split_lo(OUT0 + 2 + (1, 3, 5, 6).index(r))
            split_lo(OUT0 + 6)
            ret_center(k)
            ret_variance(k)
            ret_norm(k)
            split_lo(OUT0 + 7)
            split_lo(OUT0 + 8)
            ret_gate(k)
            ret_low(k)
            split_lo(OUT0 + 9)

            def out_residual(s):
                if s == 0:
                    dve.wait_ge(gains1_loaded, 16)
                dve.wait_ge(o_rstd, s + 1)
                if s >= 2:
                    dve.wait_ge(x_added, s - 1)
                for half in range(2):
                    nc.vector.scalar_tensor_tensor(orow[:, s % 2, half * 512:half * 512 + 512], bank[O_BANK[s][half]][:],
                                                   rstd[:, 8 + s:9 + s], gains[:, 1, half * 512:half * 512 + 512],
                                                   ALU.mult, ALU.mult).then_inc(o_scaled, 1)
                dve.wait_ge(o_scaled, 2 * s + 2)
                nc.vector.tensor_tensor(xs[:, s, :], xs[:, s, :], orow[:, s % 2, :], ALU.add).then_inc(x_added, 1)

            dve.wait_ge(gains2_loaded, 16)
            for k in range(KT):
                if k == 0:
                    out_residual(0)
                if k == 1:
                    out_residual(1)
                if k == 3:
                    normed_rows(ST)
                if k == 4:
                    normed_rows(ST + 1)
                if k == 5:
                    h_low(ST)
                if k == 7:
                    h_low(ST + 1)
                split_lo(OUT0 + KT + k + 2)
            split_lo(UP0 + 2)
            out_residual(2)
            split_lo(UP0 + 3)
            out_residual(3)
            normed_rows(ST + 2)
            normed_rows(ST + 3)
            h_low(ST + 2)
            h_low(ST + 3)

            def up_post(i, j):
                t = 2 * i + ((FT if j % 2 else 0) + j // 2)
                c = (cb if j % 2 else ca)[:, j // 2, :]

                def col(tap):
                    a = 2 * FT * tap + t
                    return conv[:, a:a + 1] if isinstance(a, int) else conv[:, bass.ds(a, 1)]
                dve.wait_ge(tap2, 4 * i + (j + 1))
                nc.vector.scalar_tensor_tensor(c[:, 1:SEQ], bank[UP_BANK[j]][:, 0:SEQ - 1], col(1), c[:, 1:SEQ],
                                               ALU.mult, ALU.add).then_inc(tap1, 1)
                dve.wait_ge(tap1, 4 * i + (j + 1))
                nc.vector.scalar_tensor_tensor(c[:, 2:SEQ], bank[UP_BANK[j]][:, 0:SEQ - 2], col(0), c[:, 2:SEQ],
                                               ALU.mult, ALU.add).then_inc(tap0, 1)
                if j % 2:
                    pair = 2 * i + j // 2
                    dst = (fT[:, pair, :] if isinstance(pair, int)
                           else fT[:, bass.ds(pair, 1), :].rearrange("p o c -> p (o c)"))
                    dve.wait_ge(gelu_done, 2 * i + (j // 2 + 1))
                    dve.wait_ge(tap0, 4 * i + (j + 1))
                    nc.vector.tensor_tensor(dst, ca[:, j // 2, :], cb[:, j // 2, :], ALU.mult).then_inc(f_ready, 1)

            def down_gain(half, s):
                dve.wait_ge(down_rows, ST * half + s + 1)
                if half == 0:
                    dve.wait_ge(o_sq, 2 * ST + s + 1)
                else:
                    dve.wait_ge(o_sq, 3 * ST + s + 1)
                nc.vector.tensor_tensor(finished(s, half), bank[DOWN_BANK[half][s]][:],
                                        gains[:, 1, half * 512:half * 512 + 512], ALU.mult).then_inc(down_gained, 1)

            def down_lo(n0, q, i):
                c = slot_of(n0 + q)
                dve.wait_ge(w_hi, 2 * i + (n0 + q + 1))
                nc.vector.tensor_tensor(ws[:, c, 1, :], raw[:, c, :], f32(ws[:, c, 0, :]), ALU.subtract).then_inc(w_lo, 1)
                for kk in range(2):
                    k = 4 * i + (2 * ((n0 - DOWN0) % SWEEP + q) + kk)
                    src = fT[:, k, :] if isinstance(k, int) else fT[:, bass.ds(k, 1), :].rearrange("p o c -> p (o c)")
                    dve.wait_ge(f_hi, 4 * i + (2 * (n0 - DOWN0 + q) + kk + 1))
                    nc.vector.tensor_tensor(yT[:, 1, 2 * c + kk, :], src, f32(yT[:, 0, 2 * c + kk, :]),
                                            ALU.subtract).then_inc(f_lo, 1)

            for j in range(4):
                if j >= 2:
                    split_lo(UP0 + 2 + j)
                up_post(0, j)
            with dve.Fori(1, SWEEP - 1) as i:
                for j in range(4):
                    split_lo(UP0 + 2 + j, i, 4)
                    up_post(i, j)
            for j in range(4):
                if j < 2:
                    split_lo(UP0 + 2 + j, SWEEP - 1, 4)
                else:
                    down_lo(DOWN0, j - 2, 0)
                up_post(SWEEP - 1, j)
            for sweep in range(2):
                first = DOWN0 + sweep * SWEEP
                if sweep:
                    for q in range(2):
                        down_lo(first, q, 0)
                    dve.wait_ge(gains3_loaded, 16)
                    for s in range(ST):
                        down_gain(0, s)
                with dve.Fori(1, SWEEP // 2) as i:
                    for q in range(2):
                        down_lo(first, q, i)
                down_lo(first + SWEEP - 1, 0, 0)

            def down_residual(s):
                dve.wait_ge(o_rstd, ST + s + 1)
                dve.wait_ge(down_gained, ST + s + 1)
                for half in range(2):
                    nc.vector.scalar_tensor_tensor(finished(s, half), finished(s, half), rstd[:, 12 + s:13 + s],
                                                   xs[:, s, half * 512:half * 512 + 512],
                                                   ALU.mult, ALU.add).then_inc(down_added, 1)

            down_gain(1, 0)
            for s in range(ST):
                if s + 1 < ST:
                    down_gain(1, s + 1)
                down_residual(s)


def rotary_table():
    inv = np.float32(10000.0) ** (-np.arange(0, HD, 2, dtype=np.float32) / np.float32(HD))
    ang = (np.arange(SEQ, dtype=np.float32)[None, :] * inv.astype(np.float32)[:, None]).astype(np.float64)
    cos = np.tile(np.cos(ang), (4, 1))
    sin = np.concatenate([-np.sin(ang), np.sin(ang)] * 2, axis=0)
    return np.stack([cos, sin], axis=1).astype(np.float32)


def decay_vectors():
    gamma = 1.0 - 2.0 ** (-5.0 - np.arange(HEADS, dtype=np.float64))
    dist = np.arange(VEC) - (P - 1)
    return np.where(dist >= 0, gamma[:, None] ** np.maximum(dist, 0), 0.0).astype(np.float32) * np.float32(HD ** -0.5)


def bucket_onehot():
    dist = np.arange(VEC) - (P - 1)
    exact = BUCKETS // 2
    far = np.maximum(dist, 1).astype(np.float64)
    large = exact + np.floor(np.log(far / exact) / math.log(MAX_DIST / exact) * (BUCKETS - exact) + 1e-9).astype(np.int64)
    bucket = np.where(dist < exact, dist, np.minimum(large, BUCKETS - 1))
    bucket = np.where(dist < 0, BUCKETS, bucket)
    return (np.arange(BUCKETS + 1)[:, None] == bucket[None, :]).astype(np.float32)


_INS = ["x", "norm_mix_pre", "w_in", "rel_bias", "w_out", "norm_mix_post", "norm_ffn_pre", "w_up",
        "conv_w", "conv_b", "w_down", "norm_ffn_post"]


def kernel(**inputs):
    import numpy as _np
    import concourse.bacc as _bacc
    from concourse import mybir as _mybir
    from concourse.bass_utils import run_bass_kernel_spmd as _run

    nc = _bacc.Bacc("TRN2", target_bir_lowering=False, num_devices=1)
    arrays, args = {}, []
    given = [(name, _np.ascontiguousarray(inputs[name])) for name in _INS]
    given += [("rotary", rotary_table()), ("decay", decay_vectors()), ("onehot", bucket_onehot())]
    for name, a in given:
        arrays[f"in_{name}_dram"] = a
        args.append(nc.dram_tensor(f"in_{name}_dram", a.shape, _mybir.dt.from_np(a.dtype), kind="ExternalInput").ap())
    args.append(nc.dram_tensor("out_0_dram", (1, SEQ, D), _mybir.dt.float32, kind="ExternalOutput").ap())
    build(nc, *args)
    r = _run(nc, [arrays], core_ids=[0])
    return r.results[0]["out_0_dram"]
```

```python
import math
from contextlib import ExitStack

import concourse.bass as bass
import numpy as np
from concourse import mybir

F32 = mybir.dt.float32
F32R = mybir.dt.float32r
ALU = mybir.AluOpType
ACT = mybir.ActivationFunctionType
AX = mybir.AxisListType

P = 128
SEQ, D = 512, 1024
HD = 64
HEADS = 8
DMIX = HEADS * HD
PAIRS = HEADS // 2
DFF = 2816
FT = DFF // P
KT = D // P
ST = SEQ // P
EPS = 1e-6
BUCKETS, MAX_DIST = 32, 128
VEC = SEQ + P
GROUPS = [1, 0, 2, 4, 3, 5, 6]
KA, QA, VA, KR, QR, VR, GR = range(7)
NU = 7
OUT0 = NU * PAIRS
UP0 = OUT0 + 2 * KT
DOWN0 = UP0 + 2 * FT
SWEEP = FT // 2
LAST_UNIT = DOWN0 + 2 * SWEEP
SLOTS = 4


def slot_of(n):
    if n < OUT0:
        return n % NU % SLOTS
    if n < DOWN0:
        return (n - OUT0) % SLOTS
    sweep, k = divmod(n - DOWN0, SWEEP)
    return 2 if k == SWEEP - 1 else (0, 1, 3, 0)[2 * sweep + k % 2]


def loads_of_slot(n):
    return sum(slot_of(m) == slot_of(n) for m in range(n + 1))


def freed_at(n):
    return max((m + 1 for m in range(n) if slot_of(m) == slot_of(n)), default=0)


POOL_TO = OUT0 + 2


def lo_count(n):
    if n < POOL_TO:
        return n + 1
    return n + 1 - POOL_TO


def at_turn(f, n, i, per_turn):
    if isinstance(i, int):
        return f(n + i * per_turn)
    a, b = f(n + per_turn), f(n + 2 * per_turn)
    return (b - a) * i + (2 * a - b)


def window(dram, head, rows):
    return bass.AP(dram, head * VEC, [[1, P], [VEC, rows], [1, SEQ]])


def build(nc, x, norm_mix_pre, w_in, rel_bias, w_out, norm_mix_post, norm_ffn_pre, w_up,
          conv_w, conv_b, w_down, norm_ffn_post, rotary, decay, onehot, out):
    ctx = ExitStack()
    with ctx:
        def sb(name, shape, dt=F32):
            return ctx.enter_context(nc.sbuf_tensor(name, shape, dt))

        def sem(name):
            return ctx.enter_context(nc.semaphore(name))

        xs = sb("xs", [P, ST, D])
        hT = sb("hT", [P, 2, KT, SEQ], F32R)
        yT = sb("yT", [P, 2, KT, SEQ], F32R)
        ws = sb("ws", [P, SLOTS, 2, D], F32R)
        raw = sb("raw", [P, SLOTS, D])
        gains = sb("gains", [P, 2, D])
        ident = sb("ident", [P, P])
        rot = sb("rot", [P, 2, SEQ])
        conv = sb("conv", [P, 4 * 2 * FT])
        relb = sb("relb", [BUCKETS + 1, HEADS])
        qsA = sb("qsA", [P, 2, SEQ], F32R)
        ksA = sb("ksA", [P, 2, SEQ], F32R)
        klA = sb("klA", [P, SEQ], F32R)
        qsR = sb("qsR", [P, 2, SEQ], F32R)
        ksR = sb("ksR", [P, 2, SEQ], F32R)
        klR = sb("klR", [P, SEQ], F32R)
        neghalf = sb("neghalf", [P, 8])
        sumsq = sb("sumsq", [P, 2 * ST])
        meansq = sb("meansq", [P, 4 * ST])
        rstd = sb("rstd", [P, 4 * ST])
        osum = sb("osum", [P, 2 * ST, 2])
        negmax = sb("negmax", [P, HEADS])
        rowsum = sb("rowsum", [P, HEADS])
        rowinv = sb("rowinv", [P, HEADS])
        gsum = sb("gsum", [P, HEADS])
        gneg = sb("gneg", [P, HEADS])
        gvar = sb("gvar", [P, HEADS])
        gms = sb("gms", [P, HEADS])
        grstd = sb("grstd", [P, HEADS])
        work = sb("work", [P, 11776])

        def part(at, n):
            return work[:, at:at + n]

        vA = part(0, 512)
        vArow = part(512, 512).rearrange("p (t c) -> p t c", t=ST)
        probs = part(1024, 1536).rearrange("p (r c) -> p r c", r=3)
        probsT = part(2560, 1024).rearrange("p (r c) -> p r c", r=2)
        vR = part(3584, 512)
        vRrow = part(4096, 512).rearrange("p (t c) -> p t c", t=ST)
        gate = part(4608, 512)
        rotc, rots = part(5120, 512), part(5632, 512)
        retp = part(6144, 2560).rearrange("p (h c) -> p h c", h=2)
        centered, squares = part(8704, 512), part(9216, 512)
        gated = squares
        btab = part(9728, 1024).rearrange("p (h c) -> p h c", h=2)
        dtab = part(10752, 1024).rearrange("p (h c) -> p h c", h=2)
        oneh = work[0:BUCKETS + 1, 6144:6144 + VEC]
        bvec = work[0:HEADS, 6784:6784 + VEC]
        convrows = work[0:2 * FT, 7424:7936].rearrange("t (j p) -> t j p", j=4)
        hrow = part(0, 2048).rearrange("p (r c) -> p r c", r=2)
        orow = part(2048, 2048).rearrange("p (r c) -> p r c", r=2)
        junk = part(4096, 1024)
        ojunk = part(6144, 512)
        fT = part(0, FT * SEQ).rearrange("p (t c) -> p t c", t=FT)
        ca = rot
        cb = gains[:, 0, :].rearrange("p (r c) -> p r c", r=2)
        djunk = part(FT * SEQ, 512)
        done1 = part(0, 2048).rearrange("p (s c) -> p s c", s=ST)

        def finished(s, half):
            return done1[:, s, :] if half else (ca if s < 2 else cb)[:, s % 2, :]

        bank = [ctx.enter_context(nc.psum_tensor(f"bank{b}", [P, 512], F32)) for b in range(8)]
        UNIT_BANK = [0, 1, 0, 1, 0, 1, 7]
        S_BANK, T_BANK, YA_BANK, YR_BANK = (2, 3), (4, 5), 6, 7
        O_BANK = [(0, 1), (5, 6), (2, 3), (4, 7)]
        H_BANK = [(2, 3), (4, 5), (6, 7), (2, 3)] + O_BANK
        UP_BANK = [0, 1, 5, 6]
        DOWN_BANK = [(2, 3, 4, 7), (0, 1, 5, 6)]

        x_loaded = [sem(f"x_loaded{s}") for s in range(ST)]
        raw_loaded = [sem(f"raw_loaded{s}") for s in range(SLOTS)]
        norm1_gain_loaded = sem("norm1_gain_loaded")
        mix_post_gain_loaded = sem("mix_post_gain_loaded")
        load_granted, bias_granted = sem("load_granted"), sem("bias_granted")
        norm2_gain_loaded = sem("norm2_gain_loaded")
        ffn_post_gain_loaded = sem("ffn_post_gain_loaded")
        relb_loaded, oneh_loaded = sem("relb_loaded"), sem("oneh_loaded")
        taps_loaded, cbias_loaded = sem("taps_loaded"), sem("cbias_loaded")
        rot_loaded = sem("rot_loaded")
        btab_loaded, dtab_loaded = sem("btab_loaded"), sem("dtab_loaded")
        bvec_stored = sem("bvec_stored")
        out_stored = sem("out_stored")
        const_set = sem("const_set")
        ident_set = sem("ident_set")
        conv_turned, conv_ready = sem("conv_turned"), sem("conv_ready")
        bvec_made, bvec_ready = sem("bvec_made"), sem("bvec_ready")
        sq_done, ms_done, rstd_done = sem("sq_done"), sem("ms_done"), sem("rstd_done")
        h_rows, h_turned = sem("h_rows"), sem("h_turned")
        h_hi, h_lo = sem("h_hi"), sem("h_lo")
        w_hi, w_lo, w_lo_pool, unit_done = sem("w_hi"), sem("w_lo"), sem("w_lo_pool"), sem("unit_done")

        def lo_sem(n):
            return w_lo_pool if n < POOL_TO else w_lo

        evacuated = sem("evacuated")
        swapped, cos_done, sin_done, rotated = sem("swapped"), sem("cos_done"), sem("sin_done"), sem("rotated")
        gate_tanh, gate_sigmoid, gate_ready = sem("gate_tanh"), sem("gate_sigmoid"), sem("gate_ready")
        aq_double, rq_double = sem("aq_double"), sem("rq_double")
        aq_hi, aq_lo, rq_hi, rq_lo = sem("aq_hi"), sem("aq_lo"), sem("rq_hi"), sem("rq_lo")
        vA_turned, vA_ready = sem("vA_turned"), sem("vA_ready")
        a_scores, a_biased, a_exp, a_inv = sem("a_scores"), sem("a_biased"), sem("a_exp"), sem("a_inv")
        a_probs, a_turned, a_probsT, a_pv = sem("a_probs"), sem("a_turned"), sem("a_probsT"), sem("a_pv")
        a_yhi, a_ylo = sem("a_yhi"), sem("a_ylo")
        vR_turned, vR_ready = sem("vR_turned"), sem("vR_ready")
        r_scores, r_decayed, r_pv = sem("r_scores"), sem("r_decayed"), sem("r_pv")
        r_copied, r_rows = sem("r_copied"), sem("r_rows")
        r_sum, r_neg, r_centered, r_sq = sem("r_sum"), sem("r_neg"), sem("r_centered"), sem("r_sq")
        r_var, r_ms, r_rstd, r_normed = sem("r_var"), sem("r_ms"), sem("r_rstd"), sem("r_normed")
        r_turned, r_gated, r_yhi, r_ylo = sem("r_turned"), sem("r_gated"), sem("r_yhi"), sem("r_ylo")
        o_rows, o_gained = sem("o_rows"), sem("o_gained")
        o_sq, o_ms, o_rstd = sem("o_sq"), sem("o_ms"), sem("o_rstd")
        x_added = sem("x_added")
        tap2, tap1, tap0 = sem("tap2"), sem("tap1"), sem("tap0")
        gelu_done, f_ready = sem("gelu_done"), sem("f_ready")
        f_hi, f_lo = sem("f_hi"), sem("f_lo")
        down_rows, down_gained, down_added = sem("down_rows"), sem("down_gained"), sem("down_added")
        block = ctx.enter_context(nc.Block())

        w_in_v = w_in[0].rearrange("(k p) n -> p k n", p=P)
        w_up_v = w_up[0].rearrange("(k p) n -> p k n", p=P)
        w_out_v = w_out[0].rearrange("(k p) n -> p k n", p=P)
        w_down_v = w_down[0].rearrange("(k p) n -> p k n", p=P)
        bias_dram = nc.dram_tensor("bias_vectors", (HEADS, VEC), F32, kind="Internal")

        def width(t):
            return P * (t + 1)

        def packed(mt):
            return P * mt * (mt + 1) // 2

        @block.sync
        def _(sp):
            def load_x(s):
                sp.dma_start(xs[:, s, :], x[0, s * P:(s + 1) * P, :]).then_inc(x_loaded[s], 16)

            def load(n, i, per_turn, source, k_major=True):
                c = slot_of(n)
                if not (isinstance(i, int) and freed_at(n + i * per_turn) == 0):
                    m = n if isinstance(i, int) else n + per_turn
                    last_unit = freed_at(m + (i * per_turn if isinstance(i, int) else 0)) - 1
                    sp.wait_ge(lo_sem(last_unit), at_turn(lambda k: lo_count(freed_at(k) - 1), n, i, per_turn))
                    if not isinstance(i, int):
                        sp.sem_inc(load_granted, 1)
                dst = raw[:, c, :]
                if k_major:
                    dst = dst.rearrange("p (k n) -> p k n", n=source.shape[-1])
                sp.dma_start(dst, source).then_inc(raw_loaded[c], 16)

            def load_turn(i, j0=0, j1=NU):
                for j in range(j0, j1):
                    load(j, i, NU, w_in_v[:, :, bass.ds(GROUPS[j] * DMIX + i * P, P)])

            load_x(0)
            load_x(1)
            sp.dma_start(gains[:, 0, :], norm_mix_pre[0].partition_broadcast(P)).then_inc(norm1_gain_loaded, 16)
            load_turn(0, 0, 1)
            load_x(2)
            load_turn(0, 1, 2)
            load_x(3)
            sp.wait_ge(const_set, 2)
            sp.dma_start(relb[0:BUCKETS, :], rel_bias).then_inc(relb_loaded, 16)
            sp.dma_start(oneh, onehot).then_inc(oneh_loaded, 16)
            sp.dma_start(convrows[:, 0:3, :], conv_w[0].rearrange("j (t p) -> t j p", p=P)).then_inc(taps_loaded, 16)
            sp.dma_start(convrows[:, 3, :], conv_b[0].rearrange("(t p) -> t p", p=P)).then_inc(cbias_loaded, 16)
            load_turn(0, 2, 4)
            sp.dma_start(rot[:], rotary).then_inc(rot_loaded, 16)
            sp.dma_start(gains[:, 1, :], norm_mix_post[0].partition_broadcast(P)).then_inc(mix_post_gain_loaded, 16)
            load_turn(0, 4, NU)
            with sp.Fori(1, PAIRS) as i:
                load_turn(i)
            for n in range(2 * KT):
                load(OUT0 + n, 0, 0, w_out_v[:, n % KT, :], k_major=False)
            with sp.Fori(0, SWEEP) as i:
                for j in range(4):
                    side, half = j % 2, j // 2
                    load(UP0 + j, i, 4, w_up_v[:, :, bass.ds(side * DFF + half * P + i * (2 * P), P)])
            for sweep in range(2):
                cols = slice(sweep * 512, sweep * 512 + 512)
                first = DOWN0 + sweep * SWEEP
                for q in range(2):
                    load(first + q, 0, 2, w_down_v[:, 2 * q:2 * q + 2, cols])
                with sp.Fori(1, SWEEP // 2) as i:
                    for q in range(2):
                        load(first + q, i, 2, w_down_v[:, bass.ds(2 * q + 4 * i, 2), cols])
                load(first + SWEEP - 1, 0, 0, w_down_v[:, FT - 2:FT, cols])
            for s in range(ST):
                for half in range(2):
                    sp.wait_ge(down_added, 2 * s + half + 1)
                    sp.dma_start(out[0, s * P:(s + 1) * P, half * 512:half * 512 + 512],
                                 finished(s, half)).then_inc(out_stored, 16)
            sp.wait_ge(out_stored, 16 * 2 * ST)

        @block.gpsimd
        def _(pool):
            pool.memset(neghalf[:], -0.5).then_inc(const_set, 1)
            pool.wait_ge(const_set, 1)
            pool.memset(relb[BUCKETS:BUCKETS + 1, :], -1e30).then_inc(const_set, 1)
            pool.wait_ge(const_set, 2)
            pool.memset(ident[:], 0.0).then_inc(ident_set, 1)
            pool.wait_ge(ident_set, 1)
            pool.affine_select(out=ident[:], in_=ident[:], compare_op=ALU.not_equal, fill=1.0, base=0,
                               pattern=[[-1, P]], channel_multiplier=1).then_inc(ident_set, 1)
            pool.wait_ge(ident_set, 2)

            def row_rstd(t, src):
                nc.gpsimd.tensor_scalar(meansq[:, t:t + 1], src, 1.0 / D, EPS, ALU.mult, ALU.add).then_inc(ms_done, 1)
                pool.wait_ge(ms_done, t + 1)
                nc.gpsimd.tensor_tensor(rstd[:, t:t + 1], meansq[:, t:t + 1], neghalf[:, 0:1], ALU.pow).then_inc(rstd_done, 1)

            def out_rstd(t):
                pool.wait_ge(o_sq, 2 * t + 2 if t < ST else 2 * ST + t + 1)
                nc.gpsimd.tensor_scalar(meansq[:, 8 + t:9 + t], osum[:, t, 0:1], osum[:, t, 1:2], EPS,
                                        ALU.add, ALU.add).then_inc(o_ms, 1)
                pool.wait_ge(o_ms, t + 1)
                nc.gpsimd.tensor_tensor(rstd[:, 8 + t:9 + t], meansq[:, 8 + t:9 + t], neghalf[:, 0:1],
                                        ALU.pow).then_inc(o_rstd, 1)

            def split_lo(n):
                c = slot_of(n)
                pool.wait_ge(w_hi, n + 1)
                nc.gpsimd.tensor_tensor(ws[:, c, 1, :], raw[:, c, :], ws[:, c, 0, :].bitcast(F32),
                                        ALU.subtract).then_inc(w_lo_pool, 1)

            def x_rstd(s):
                pool.wait_ge(sq_done, s + 1)
                row_rstd(s, sumsq[:, s:s + 1])

            x_rstd(0)
            x_rstd(1)
            split_lo(0)
            x_rstd(2)
            split_lo(1)
            x_rstd(3)
            split_lo(2)
            pool.wait_ge(bvec_ready, 2)
            pool.dma_start(bias_dram[:, :], bvec[:]).then_inc(bvec_stored, 16)
            pool.wait_ge(bvec_stored, 16)

            def group_rstd(k):
                pool.wait_ge(r_var, k + 1)
                nc.gpsimd.tensor_scalar(gms[:], gvar[:], 1.0 / HD, EPS, ALU.mult, ALU.add).then_inc(r_ms, 1)
                pool.wait_ge(r_ms, k + 1)
                nc.gpsimd.tensor_tensor(grstd[:], gms[:], neghalf[:], ALU.pow).then_inc(r_rstd, 1)

            def rotary_sum(i, side):
                pool.wait_ge(sin_done, 2 * i + side + 1)
                nc.gpsimd.tensor_tensor(rotc, rotc, rots, ALU.add).then_inc(rotated, 1)

            def double_keys(keys, hi, signal, i, last_lo):
                pool.wait_ge(hi, 2 * i + 1)
                pool.wait_ge(w_lo_pool, lo_count(last_lo))
                for h in range(2):
                    own, other = slice(HD * h, HD * h + HD), slice(HD * (1 - h), HD * (1 - h) + HD)
                    nc.gpsimd.tensor_copy(keys[other, h, :], keys[own, h, :]).then_inc(signal, 1)
                    pool.wait_ge(signal, 2 * i + h + 1)

            for i in range(PAIRS):
                if i:
                    pool.wait_ge(a_biased, 8 * i)
                pool.dma_start(btab, window(bias_dram, 2 * i, 2)).then_inc(btab_loaded, 16)
                if i:
                    split_lo(NU * i + 2)
                split_lo(NU * i + 3)
                double_keys(ksA, aq_hi, aq_double, i, NU * i + 3)
                split_lo(NU * i + 4)
                if i:
                    pool.wait_ge(r_decayed, 8 * i)
                pool.dma_start(dtab, window(decay.tensor, 2 * i, 2)).then_inc(dtab_loaded, 16)
                split_lo(NU * i + 5)
                if i:
                    group_rstd(i - 1)
                rotary_sum(i, 0)
                split_lo(NU * i + 6)
                double_keys(ksR, rq_hi, rq_double, i, NU * i + 6)
                rotary_sum(i, 1)
                split_lo(NU * i + 7)
                split_lo(NU * i + 8)
            group_rstd(PAIRS - 1)
            pool.wait_ge(h_rows, ST)
            pool.dma_start(gains[:, 0, :], norm_ffn_pre[0].partition_broadcast(P)).then_inc(norm2_gain_loaded, 16)
            for pair in ((0, 1), (2, 3)):
                for s in pair:
                    out_rstd(s)
                for s in pair:
                    pool.wait_ge(sq_done, ST + s + 1)
                    row_rstd(ST + s, sumsq[:, ST + s:ST + s + 1])
            pool.wait_ge(o_gained, 2 * ST)
            pool.dma_start(gains[:, 1, :], norm_ffn_post[0].partition_broadcast(P)).then_inc(ffn_post_gain_loaded, 16)
            for s in range(ST):
                out_rstd(ST + s)

        @block.tensor
        def _(pe):
            def three(dst, st_hi, st_lo, mv_hi, mv_lo, p, start, stop):
                st, mv = ((st_hi, mv_hi), (st_hi, mv_lo), (st_lo, mv_hi))[p]
                return nc.tensor.matmul(dst, st, mv, start=start, stop=stop)

            def turn_rows(t):
                banks = H_BANK[t]
                pe.wait_ge(h_rows, t + 1)
                for half in range(2):
                    if t == 3:
                        pe.wait_ge(h_lo, 2)
                    for k in range(4):
                        c = (4 * half + k) * P
                        ins = nc.tensor.transpose(bank[banks[half]][:, k * P:(k + 1) * P],
                                                  hrow[:, t % 2, c:c + P], ident[:])
                    ins.then_inc(h_turned, 1)

            def column_unit(n, dst, m0, m1, part=slice(0, SEQ), finish=True):
                c = slot_of(n)
                for m in range(m0, m1):
                    k, p = divmod(m, 3)
                    cols = slice(k * P, (k + 1) * P)
                    ins = three(dst[:, part], ws[:, c, 0, cols], ws[:, c, 1, cols], hT[:, 0, k, part], hT[:, 1, k, part],
                                p, m == 0, m == 23)
                if m1 == 24 and finish:
                    ins.then_inc(unit_done, 1)

            def warm(n):
                for m in range(n):
                    nc.tensor.matmul(bank[0][:, 0:P], ident[:], ident[:], start=True, stop=True)

            FRONT, BACK = slice(0, SEQ // 2), slice(SEQ // 2, SEQ)

            def project(i, j, m0, m1):
                if m0 == 0:
                    pe.wait_ge(w_lo_pool, at_turn(lo_count, j, i, NU))
                    first = isinstance(i, int) and i == 0
                    if j == 0 and not first:
                        pe.wait_ge(cos_done, 2 * i)
                    if j == 1 and not first:
                        pe.wait_ge(evacuated, 2 * i)
                    if j in (2, 3):
                        pe.wait_ge(aq_lo, 2 * i + (j - 1))
                    if j == 4:
                        pe.wait_ge(evacuated, 2 * i + 1)
                    if j == 5:
                        pe.wait_ge(cos_done, 2 * i + 1)
                    if j == 6 and not first:
                        pe.wait_ge(r_gated, i)
                column_unit(j, bank[UNIT_BANK[j]], m0, m1)

            def ret_values(k):
                pe.wait_ge(evacuated, 2 * k + 2)
                pe.wait_ge(a_probsT, 8 * k + 8)
                for t in range(ST):
                    ins = nc.tensor.transpose(bank[T_BANK[0]][:, t * P:(t + 1) * P], vR[:, t * P:(t + 1) * P], ident[:])
                ins.then_inc(vR_turned, 1)

            def ret_scores(k, u):
                h, mt = u // 4, 3 - u % 4
                if u == 0:
                    pe.wait_ge(rq_lo, 2 * k + 2)
                    pe.wait_ge(rq_double, 2 * k + 2)
                    pe.wait_ge(a_biased, 8 * k + 8)
                if u >= 2:
                    pe.wait_ge(r_decayed, 8 * k + u - 1)
                rows = slice(HD * h, HD * h + HD)
                dst, tile, wide = bank[S_BANK[u % 2]][:, 0:width(mt)], slice(mt * P, (mt + 1) * P), slice(SEQ - width(mt), SEQ)
                nc.tensor.matmul(dst, ksR[:, h, tile], qsR[:, h, wide], start=True, stop=False)
                nc.tensor.matmul(dst, klR[rows, tile], qsR[rows, h, wide], start=False, stop=True).then_inc(r_scores, 1)

            def ret_mix(k, u):
                h, mt = u // 4, 3 - u % 4
                if u == 0:
                    pe.wait_ge(vR_ready, k + 1)
                    pe.wait_ge(gate_ready, k + 1)
                pe.wait_ge(r_decayed, 8 * k + u + 1)
                ins = nc.tensor.matmul(bank[YR_BANK][HD * h:HD * h + HD, SEQ - width(mt):SEQ],
                                       vRrow[:, mt, HD * h:HD * h + HD], retp[:, h, packed(mt):packed(mt) + width(mt)],
                                       start=mt == 3, stop=mt == 0)
                if u == 7:
                    ins.then_inc(r_pv, 1)

            def ret_rows(k):
                pe.wait_ge(r_copied, k + 1)
                for t in range(ST):
                    ins = nc.tensor.transpose(bank[YR_BANK][:, t * P:(t + 1) * P],
                                              centered[:, t * P:(t + 1) * P], ident[:])
                ins.then_inc(r_rows, 1)

            def ret_turn_out(k):
                pe.wait_ge(r_normed, k + 1)
                for t in range(ST):
                    ins = nc.tensor.transpose(bank[YR_BANK][:, t * P:(t + 1) * P],
                                              centered[:, t * P:(t + 1) * P], ident[:])
                ins.then_inc(r_turned, 1)

            def moba_values(i, first):
                pe.wait_ge(evacuated, 2 * i + 1)
                if first:
                    pe.wait_ge(bvec_ready, 2)
                    pe.wait_ge(conv_ready, 1)
                for t in range(ST):
                    ins = nc.tensor.transpose(bank[T_BANK[1]][:, t * P:(t + 1) * P], vA[:, t * P:(t + 1) * P], ident[:])
                ins.then_inc(vA_turned, 1)

            def moba_scores(i, u, first):
                h, qt = u // 4, u % 4
                if u == 0:
                    pe.wait_ge(aq_double, 2 * i + 2)
                    pe.wait_ge(aq_lo, 2 * i + 2)
                if u < 2 and not first:
                    pe.wait_ge(r_decayed, 8 * i)
                if u >= 2:
                    pe.wait_ge(a_biased, 8 * i + u - 1)
                rows = slice(HD * h, HD * h + HD)
                dst, tile, wide = bank[S_BANK[u % 2]][:, 0:width(qt)], slice(qt * P, (qt + 1) * P), slice(SEQ - width(qt), SEQ)
                nc.tensor.matmul(dst, qsA[:, h, tile], ksA[:, h, wide], start=True, stop=False)
                nc.tensor.matmul(dst, qsA[rows, h, tile], klA[rows, wide], start=False, stop=True).then_inc(a_scores, 1)

            def moba_turn(i, u):
                qt = u % 4
                pe.wait_ge(a_probs, 8 * i + u + 1)
                if u < 2:
                    pe.wait_ge(vA_ready, i + 1)
                else:
                    pe.wait_ge(a_probsT, 8 * i + u - 1)
                for t in range(qt + 1):
                    ins = nc.tensor.transpose(bank[T_BANK[u % 2]][:, t * P:(t + 1) * P],
                                              probs[:, u % 3, t * P:(t + 1) * P], ident[:])
                ins.then_inc(a_turned, 1)

            def moba_mix(i, u, first):
                h, qt = u // 4, u % 4
                if u == 0 and not first:
                    pe.wait_ge(a_ylo, i)
                pe.wait_ge(a_probsT, 8 * i + u + 1)
                for t in range(qt + 1):
                    ins = nc.tensor.matmul(bank[YA_BANK][HD * h:HD * h + HD, qt * P:(qt + 1) * P],
                                           vArow[:, 3 - qt + t, HD * h:HD * h + HD],
                                           probsT[:, u % 2, t * P:(t + 1) * P], start=t == 0, stop=t == qt)
                ins.then_inc(a_pv, 1)

            def mixer_turn(i, first):
                for r in range(6 if first else 0, 9):
                    project(i, r // 3, 8 * (r % 3), 8 * (r % 3) + 8)
                    if not first:
                        if r == 0:
                            ret_values(i - 1)
                        if r >= 2:
                            ret_mix(i - 1, r - 2)
                        if r < 8:
                            ret_scores(i - 1, r)
                for u in range(12):
                    project(i, 3 + u // 3, 8 * (u % 3), 8 * (u % 3) + 8)
                    if u == 0:
                        if not first:
                            ret_mix(i - 1, 7)
                        moba_values(i, first)
                    if u == 1 and not first:
                        ret_rows(i - 1)
                    if u == 6 and not first:
                        ret_turn_out(i - 1)
                    if 3 <= u < 11:
                        moba_mix(i, u - 3, first)
                    if u < 8:
                        moba_scores(i, u, first)
                    if 2 <= u < 10:
                        moba_turn(i, u - 2)

            pe.wait_ge(ident_set, 2)
            warm(15)
            turn_rows(0)
            warm(2)
            turn_rows(1)
            warm(8)
            pe.wait_ge(h_lo, 4)
            pe.wait_ge(w_lo_pool, 1)
            column_unit(0, bank[0], 0, 24, FRONT, False)
            turn_rows(2)
            pe.wait_ge(w_lo_pool, 2)
            column_unit(1, bank[1], 0, 24, FRONT, False)
            turn_rows(3)
            pe.wait_ge(taps_loaded, 16)
            pe.wait_ge(cbias_loaded, 16)
            for j in range(4):
                ins = nc.tensor.transpose(bank[4][:, j * 2 * FT:(j + 1) * 2 * FT], convrows[:, j, :],
                                          ident[0:2 * FT, 0:2 * FT])
            ins.then_inc(conv_turned, 1)
            pe.wait_ge(relb_loaded, 16)
            pe.wait_ge(oneh_loaded, 16)
            pe.wait_ge(const_set, 2)
            pe.wait_ge(h_lo, 6)
            for b, lo, hi in ((5, 0, 512), (6, 512, VEC)):
                ins = nc.tensor.matmul(bank[b][0:HEADS, 0:hi - lo], relb[:], oneh[:, lo:hi], start=True, stop=True)
            ins.then_inc(bvec_made, 1)
            pe.wait_ge(h_lo, 2 * ST)
            column_unit(0, bank[0], 0, 24, BACK)
            column_unit(1, bank[1], 0, 24, BACK)
            mixer_turn(0, True)
            with pe.Fori(1, PAIRS) as i:
                mixer_turn(i, False)

            def out_rows(pass_, m0, m1):
                for m in range(m0, m1):
                    k, r = divmod(m, 12)
                    n = OUT0 + pass_ * KT + k
                    s, half, p = 2 * pass_ + r // 6, r // 3 % 2, r % 3
                    if r == 0:
                        pe.wait_ge(lo_sem(n), lo_count(n))
                        if pass_ == 0 and k < PAIRS:
                            pe.wait_ge(a_ylo, k + 1)
                        if pass_ == 0 and k >= PAIRS:
                            pe.wait_ge(r_ylo, k - PAIRS + 1)
                    rows = slice(s * P, (s + 1) * P)
                    c = slot_of(n)
                    ins = three(bank[O_BANK[s][half]][:], yT[:, 0, k, rows], yT[:, 1, k, rows],
                                ws[:, c, 0, half * 512:half * 512 + 512], ws[:, c, 1, half * 512:half * 512 + 512],
                                p, k == 0 and p == 0, k == KT - 1 and p == 2)
                    if r == 11:
                        ins.then_inc(unit_done, 1)
                    if r == 5 and k == KT - 1:
                        ins.then_inc(o_rows, 1)

            k = PAIRS - 1
            pe.wait_ge(cos_done, 2 * PAIRS)
            pe.wait_ge(evacuated, 2 * PAIRS)
            for r in range(10):
                if r == 0:
                    ret_values(k)
                if r >= 2:
                    ret_mix(k, r - 2)
                if r < 8:
                    ret_scores(k, r)
                if r == 2:
                    pe.wait_ge(a_ylo, PAIRS)
                out_rows(0, 4 * r, 4 * r + 4)
            out_rows(0, 40, 44)
            ret_rows(k)
            out_rows(0, 44, 72)
            ret_turn_out(k)
            out_rows(0, 72, 96)
            pe.wait_ge(r_gated, PAIRS)
            pe.wait_ge(r_decayed, 8 * PAIRS)
            pe.wait_ge(vR_ready, PAIRS)
            for k in range(KT - 2):
                out_rows(1, 12 * k, 12 * k + 12)
                if k == 4:
                    turn_rows(ST)
            a, b = 12 * (KT - 2), 12 * (KT - 1)
            out_rows(1, a, a + 6)
            turn_rows(ST + 1)
            out_rows(1, b, b + 6)
            out_rows(1, a + 6, a + 12)
            out_rows(1, b + 6, b + 12)

            for j in range(4):
                if j == 0:
                    pe.wait_ge(h_lo, 2 * ST + 4)
                pe.wait_ge(w_lo, lo_count(UP0 + j))
                column_unit(UP0 + j, bank[UP_BANK[j]], 0, 12, FRONT)
                if j >= 2:
                    turn_rows(ST + j)
                column_unit(UP0 + j, bank[UP_BANK[j]], 12, 24, FRONT, False)
            pe.wait_ge(h_lo, 4 * ST)
            for j in range(4):
                column_unit(UP0 + j, bank[UP_BANK[j]], 0, 24, BACK)
            with pe.Fori(1, SWEEP) as i:
                for j in range(4):
                    pe.wait_ge(w_lo, 4 * i + lo_count(UP0 + j))
                    pe.wait_ge(tap0, 4 * i + (j - 3))
                    column_unit(UP0 + j, bank[UP_BANK[j]], 0, 24)

            def down_product(sweep, c, kk, s, start, stop):
                cols, rows = slice(kk * 512, kk * 512 + 512), slice(s * P, (s + 1) * P)
                for p in range(3):
                    ins = three(bank[DOWN_BANK[sweep][s]][:], yT[:, 0, 2 * c + kk, rows], yT[:, 1, 2 * c + kk, rows],
                                ws[:, c, 0, cols], ws[:, c, 1, cols], p, start and p == 0, stop and p == 2)
                return ins

            def down_unit(sweep, n0, q, i, start):
                pe.wait_ge(w_lo, 2 * i + lo_count(n0 + q))
                pe.wait_ge(f_lo, 4 * i + (2 * (n0 - DOWN0 + q) + 2))
                for kk in range(2):
                    for s in range(ST):
                        ins = down_product(sweep, slot_of(n0 + q), kk, s, start and kk == 0, False)
                ins.then_inc(unit_done, 1)

            for sweep in range(2):
                first = DOWN0 + sweep * SWEEP
                if sweep == 0:
                    pe.wait_ge(h_lo, 4 * ST)
                else:
                    pe.wait_ge(tap0, 2 * FT)
                for q in range(2):
                    down_unit(sweep, first, q, 0, q == 0)
                with pe.Fori(1, SWEEP // 2 - 1) as i:
                    for q in range(2):
                        down_unit(sweep, first, q, i, False)
                down_unit(sweep, first, 0, SWEEP // 2 - 1, False)
                n = first + SWEEP - 1
                for m, s in ((n - 1, 0), (n - 1, 1), (n, 0), (n, 1), (n - 1, 2), (n, 2), (n - 1, 3), (n, 3)):
                    if s == 0:
                        pe.wait_ge(w_lo, lo_count(m))
                        pe.wait_ge(f_lo, 2 * (m - DOWN0) + 2)
                    for kk in range(2):
                        ins = down_product(sweep, slot_of(m), kk, s, False, m == n and kk == 1)
                    if m == n:
                        ins.then_inc(down_rows, 1)
                    elif s == ST - 1:
                        ins.then_inc(unit_done, 1)
                pe.wait_ge(down_rows, ST * sweep + ST)
                pe.sem_inc(unit_done, 1)

        @block.scalar
        def _(act):
            def split_hi(n, i=0, per_turn=0):
                c = slot_of(n)
                act.wait_ge(raw_loaded[c], at_turn(lambda m: 16 * loads_of_slot(m), n, i, per_turn))
                if not (isinstance(i, int) and freed_at(n + i * per_turn) == 0):
                    act.wait_ge(unit_done, at_turn(freed_at, n, i, per_turn))
                nc.scalar.activation(ws[:, c, 0, :], raw[:, c, :], ACT.Copy).then_inc(w_hi, 1)

            def h_evacuate(t):
                banks = H_BANK[t]
                s = t % ST
                for half in range(2):
                    act.wait_ge(h_turned, 2 * t + half + 1)
                    nc.scalar.activation(hT[:, 0, 4 * half:4 * half + 4, s * P:(s + 1) * P],
                                         bank[banks[half]][:].rearrange("p (k c) -> p k c", k=4),
                                         ACT.Copy).then_inc(h_hi, 1)

            def row_squares(t):
                if t:
                    act.wait_ge(sq_done, t)
                nc.scalar.activation(junk, xs[:, t % ST, :], ACT.Square, accum_out=sumsq[:, t:t + 1]).then_inc(sq_done, 1)

            def x_in(s):
                act.wait_ge(x_loaded[s], 16)
                row_squares(s)

            x_in(0)
            x_in(1)
            split_hi(0)
            h_evacuate(0)
            h_evacuate(1)
            x_in(2)
            split_hi(1)
            x_in(3)
            h_evacuate(2)
            h_evacuate(3)
            split_hi(2)
            act.wait_ge(conv_turned, 1)
            nc.scalar.activation(conv[:], bank[4][:, 0:8 * FT], ACT.Copy).then_inc(conv_ready, 1)
            act.wait_ge(bvec_made, 1)
            for b, lo, hi in ((5, 0, 512), (6, 512, VEC)):
                nc.scalar.activation(bvec[:, lo:hi], bank[b][0:HEADS, 0:hi - lo], ACT.Copy, scale=8.0).then_inc(bvec_ready, 1)

            def stack_hi(src, keys, queries, side, signal):
                for h in range(2):
                    own = slice(HD * h, HD * h + HD)
                    if side == 0:
                        ins = nc.scalar.activation(keys[own, h, ::-1], src[own, :], ACT.Copy)
                    else:
                        ins = nc.scalar.activation(queries[own, h, :], src[own, :], ACT.Copy)
                ins.then_inc(signal, 1)

            def evacuate(i, j, dst):
                act.wait_ge(unit_done, at_turn(lambda n: n + 1, j, i, NU))
                nc.scalar.activation(dst, bank[UNIT_BANK[j]][:], ACT.Copy).then_inc(evacuated, 1)

            def swap_halves(i, j, first):
                act.wait_ge(unit_done, at_turn(lambda n: n + 1, j, i, NU))
                if j == QR or not first:
                    act.wait_ge(rotated, 2 * i + (j - KR))
                for b in range(4):
                    src = 32 * (b ^ 1)
                    ins = nc.scalar.activation(rots[32 * b:32 * b + 32, :], bank[UNIT_BANK[j]][src:src + 32, :], ACT.Copy)
                ins.then_inc(swapped, 1)

            def gate_halftanh(k):
                act.wait_ge(unit_done, at_turn(lambda n: n + 1, GR, k, NU))
                nc.scalar.activation(gate, bank[UNIT_BANK[GR]][:], ACT.Tanh, scale=0.5).then_inc(gate_tanh, 1)

            def ret_copy(k):
                act.wait_ge(r_pv, k + 1)
                nc.scalar.activation(centered, bank[YR_BANK][:], ACT.Copy).then_inc(r_copied, 1)

            def moba_stack(i, side, first):
                act.wait_ge(unit_done, at_turn(lambda n: n + 1, KA + side, i, NU))
                if not first:
                    act.wait_ge(a_scores, 8 * i)
                stack_hi(bank[UNIT_BANK[KA + side]], ksA, qsA, side, aq_hi)

            def ret_stack(i, side, first):
                act.wait_ge(rotated, 2 * i + side + 1)
                if not first:
                    act.wait_ge(r_scores, 8 * i)
                stack_hi(rotc, ksR, qsR, side, rq_hi)

            def mixer_turn(i, first):
                for r in range(9):
                    if r == 0 and not first:
                        gate_halftanh(i - 1)
                        act.wait_ge(vR_turned, i)
                        nc.scalar.activation(vRrow, bank[T_BANK[0]][:].rearrange("p (t c) -> p t c", t=ST),
                                             ACT.Copy).then_inc(vR_ready, 1)
                    if r == 3:
                        moba_stack(i, 0, first)
                    if r == 6:
                        moba_stack(i, 1, first)
                    if r % 3 == 1 and not (r == 1 and first):
                        split_hi(r // 3 + 2, i, NU)
                for u in range(12):
                    if u == 0:
                        evacuate(i, VA, vA[:, ::-1])
                    if u == 1 and not first:
                        ret_copy(i - 1)
                    if u == 1:
                        if not first:
                            act.wait_ge(a_pv, 8 * i)
                        act.wait_ge(vA_turned, i + 1)
                        nc.scalar.activation(vArow, bank[T_BANK[1]][:].rearrange("p (t c) -> p t c", t=ST),
                                             ACT.Copy).then_inc(vA_ready, 1)
                    if 2 <= u < 10:
                        v = u - 2
                        w = width(v % 4)
                        act.wait_ge(a_turned, 8 * i + v + 1)
                        if v >= 2:
                            act.wait_ge(a_pv, 8 * i + v - 1)
                        nc.scalar.activation(probsT[:, v % 2, 0:w], bank[T_BANK[v % 2]][:, 0:w],
                                             ACT.Copy).then_inc(a_probsT, 1)
                    if u < 8:
                        w = width(u % 4)
                        act.wait_ge(a_biased, 8 * i + u + 1)
                        nc.scalar.activation(probs[:, u % 3, 0:w], probs[:, u % 3, 0:w], ACT.Exp, scale=-1.0,
                                             bias=negmax[:, u:u + 1], accum_out=rowsum[:, u:u + 1]).then_inc(a_exp, 1)
                    if u == 3 and not first:
                        act.wait_ge(r_centered, i)
                        nc.scalar.activation(squares, centered, ACT.Square).then_inc(r_sq, 1)
                    if u == 3:
                        swap_halves(i, KR, first)
                    if u == 6:
                        swap_halves(i, QR, first)
                    if u == 7 and not first:
                        act.wait_ge(r_gated, i)
                        nc.scalar.activation(yT[:, 0, i + (PAIRS - 1), :] if isinstance(i, int)
                                             else yT[:, 0, bass.ds(i + (PAIRS - 1), 1), :].rearrange("p o c -> p (o c)"),
                                             gated, ACT.Copy).then_inc(r_yhi, 1)
                    if u == 9:
                        evacuate(i, VR, vR[:, ::-1])
                    if u == 5:
                        ret_stack(i, 0, first)
                    if u == 9:
                        ret_stack(i, 1, first)
                    if u % 3 == 1:
                        split_hi(u // 3 + 5, i, NU)
                act.wait_ge(a_pv, 8 * i + 8)
                nc.scalar.activation(yT[:, 0, i, :] if isinstance(i, int)
                                     else yT[:, 0, bass.ds(i, 1), :].rearrange("p o c -> p (o c)"),
                                     bank[YA_BANK][:], ACT.Copy).then_inc(a_yhi, 1)

            mixer_turn(0, True)
            with act.Fori(1, PAIRS) as i:
                mixer_turn(i, False)

            k = PAIRS - 1
            gate_halftanh(k)
            act.wait_ge(vR_turned, PAIRS)
            nc.scalar.activation(vRrow, bank[T_BANK[0]][:].rearrange("p (t c) -> p t c", t=ST), ACT.Copy).then_inc(vR_ready, 1)
            for n in range(2, 6):
                split_hi(OUT0 + n)
            ret_copy(k)
            split_hi(OUT0 + 6)
            split_hi(OUT0 + 7)
            act.wait_ge(r_centered, PAIRS)
            nc.scalar.activation(squares, centered, ACT.Square).then_inc(r_sq, 1)
            split_hi(OUT0 + 8)
            act.wait_ge(r_gated, PAIRS)
            nc.scalar.activation(yT[:, 0, KT - 1, :], gated, ACT.Copy).then_inc(r_yhi, 1)
            split_hi(OUT0 + 9)

            def out_squares(s):
                for half in range(2):
                    if s or half:
                        act.wait_ge(o_sq, 2 * s + half)
                    nc.scalar.activation(ojunk, bank[O_BANK[s][half]][:], ACT.Square, scale=D ** -0.5,
                                         accum_out=osum[:, s, half:half + 1]).then_inc(o_sq, 1)

            def x_squares(s):
                act.wait_ge(x_added, 2 * s + 2)
                row_squares(ST + s)

            for k in range(KT):
                split_hi(OUT0 + KT + k + 2)
                if k == 0:
                    act.wait_ge(o_rows, 1)
                    out_squares(0)
                    act.wait_ge(unit_done, OUT0 + KT)
                    out_squares(1)
                if k == 2:
                    x_squares(0)
                if k == 3:
                    x_squares(1)
                if k == 5:
                    h_evacuate(ST)
                if k == 7:
                    h_evacuate(ST + 1)
            act.wait_ge(o_rows, 2)
            out_squares(2)
            split_hi(UP0 + 2)
            act.wait_ge(unit_done, UP0)
            out_squares(3)
            x_squares(2)
            split_hi(UP0 + 3)
            x_squares(3)
            for s in (2, 3):
                h_evacuate(ST + s)

            def up_post(i, j, first):
                t = 2 * i + ((FT if j % 2 else 0) + j // 2)
                dst = (cb if j % 2 else ca)[:, j // 2, :]
                act.wait_ge(unit_done, 4 * i + (UP0 + j + 1))
                if not first:
                    act.wait_ge(f_ready, 2 * i + (j // 2 - 1))
                def col(tap):
                    c = 2 * FT * tap + t
                    return conv[:, c:c + 1] if isinstance(c, int) else conv[:, bass.ds(c, 1)]
                nc.scalar.activation(dst, bank[UP_BANK[j]][:], ACT.Identity, scale=col(2), bias=col(3)).then_inc(tap2, 1)
                if j % 2:
                    act.wait_ge(tap0, 4 * i + j)
                    nc.scalar.activation(ca[:, j // 2, :], ca[:, j // 2, :], ACT.Gelu_apprx_tanh).then_inc(gelu_done, 1)

            def f_split_hi(n0, q, i):
                for kk in range(2):
                    k0 = 2 * ((n0 - DOWN0) % SWEEP + q) + kk
                    k = 4 * i + k0
                    src = fT[:, k, :] if isinstance(k, int) else fT[:, bass.ds(k, 1), :].rearrange("p o c -> p (o c)")
                    nc.scalar.activation(yT[:, 0, 2 * slot_of(n0 + q) + kk, :], src, ACT.Copy).then_inc(f_hi, 1)

            def down_squares(sweep):
                for s in range(ST):
                    act.wait_ge(down_rows, ST * sweep + s + 1)
                    act.wait_ge(o_sq, 2 * ST + ST * sweep + s)
                    nc.scalar.activation(djunk, bank[DOWN_BANK[sweep][s]][:], ACT.Square, scale=D ** -0.5,
                                         accum_out=osum[:, ST + s, sweep:sweep + 1]).then_inc(o_sq, 1)

            def down_hi(n0, q, i):
                c = slot_of(n0 + q)
                act.wait_ge(raw_loaded[c], 16 * i + 16 * loads_of_slot(n0 + q))
                act.wait_ge(unit_done, at_turn(freed_at, n0 + q, i, 2))
                nc.scalar.activation(ws[:, c, 0, :], raw[:, c, :], ACT.Copy).then_inc(w_hi, 1)
                f_split_hi(n0, q, i)

            for j in range(4):
                if j >= 2:
                    split_hi(UP0 + 2 + j)
                up_post(0, j, True)
            with act.Fori(1, SWEEP - 1) as i:
                for j in range(4):
                    split_hi(UP0 + 2 + j, i, 4)
                    up_post(i, j, False)
            for j in range(4):
                if j < 2:
                    split_hi(UP0 + 2 + j, SWEEP - 1, 4)
                else:
                    down_hi(DOWN0, j - 2, 0)
                up_post(SWEEP - 1, j, False)
            for sweep in range(2):
                first = DOWN0 + sweep * SWEEP
                if sweep:
                    for q in range(2):
                        down_hi(first, q, 0)
                    down_squares(0)
                with act.Fori(1, SWEEP // 2) as i:
                    for q in range(2):
                        down_hi(first, q, i)
                if sweep == 0:
                    act.wait_ge(f_ready, FT)
                down_hi(first + SWEEP - 1, 0, 0)
            down_squares(1)

        @block.vector
        def _(dve):
            def f32(ap):
                return ap.bitcast(F32)

            def split_lo(n, i=0, per_turn=0):
                c = slot_of(n)
                dve.wait_ge(w_hi, at_turn(lambda m: m + 1, n, i, per_turn))
                nc.vector.tensor_tensor(ws[:, c, 1, :], raw[:, c, :], f32(ws[:, c, 0, :]), ALU.subtract).then_inc(w_lo, 1)

            def normed_rows(t):
                dve.wait_ge(rstd_done, t + 1)
                if t >= 2:
                    dve.wait_ge(h_turned, 2 * (t - 1))
                nc.vector.scalar_tensor_tensor(hrow[:, t % 2, :], xs[:, t % ST, :], rstd[:, t:t + 1],
                                               gains[:, 0, :], ALU.mult, ALU.mult).then_inc(h_rows, 1)

            def h_low(t):
                banks = H_BANK[t]
                s = t % ST
                for half in range(2):
                    dve.wait_ge(h_hi, 2 * t + half + 1)
                    cols = (slice(None), slice(4 * half, 4 * half + 4), slice(s * P, (s + 1) * P))
                    nc.vector.tensor_tensor(hT[:, 1, 4 * half:4 * half + 4, s * P:(s + 1) * P],
                                            bank[banks[half]][:].rearrange("p (k c) -> p k c", k=4),
                                            f32(hT[:, 0, 4 * half:4 * half + 4, s * P:(s + 1) * P]),
                                            ALU.subtract).then_inc(h_lo, 1)

            dve.wait_ge(norm1_gain_loaded, 16)
            normed_rows(0)
            normed_rows(1)
            h_low(0)
            h_low(1)
            normed_rows(2)
            normed_rows(3)
            h_low(2)
            h_low(3)
            dve.wait_ge(rot_loaded, 16)

            def gate_finish(k):
                dve.wait_ge(gate_tanh, k + 1)
                nc.vector.tensor_scalar(gate, gate, 0.5, 0.5, ALU.mult, ALU.add).then_inc(gate_sigmoid, 1)
                dve.wait_ge(gate_sigmoid, k + 1)
                nc.vector.tensor_tensor(gate, bank[UNIT_BANK[GR]][:], gate, ALU.mult).then_inc(gate_ready, 1)

            def stack_lo(src, keys, keys_lo, queries, side, signal):
                for h in range(2):
                    own, other = slice(HD * h, HD * h + HD), slice(HD * (1 - h), HD * (1 - h) + HD)
                    if side == 0:
                        ins = nc.vector.tensor_tensor(keys_lo[own, ::-1], src[own, :], f32(keys[own, h, ::-1]), ALU.subtract)
                    else:
                        ins = nc.vector.tensor_tensor(queries[other, h, :], src[own, :], f32(queries[own, h, :]), ALU.subtract)
                ins.then_inc(signal, 1)

            def moba_stack(i, side):
                dve.wait_ge(aq_hi, 2 * i + side + 1)
                stack_lo(bank[UNIT_BANK[KA + side]], ksA, klA, qsA, side, aq_lo)

            def ret_stack(i, side):
                dve.wait_ge(rq_hi, 2 * i + side + 1)
                stack_lo(rotc, ksR, klR, qsR, side, rq_lo)

            def ret_decay(k, u):
                h, mt = u // 4, 3 - u % 4
                if u == 0:
                    dve.wait_ge(dtab_loaded, 16 * k + 16)
                dve.wait_ge(r_scores, 8 * k + u + 1)
                nc.vector.tensor_tensor(retp[:, h, packed(mt):packed(mt) + width(mt)],
                                        bank[S_BANK[u % 2]][:, 0:width(mt)], dtab[:, h, 0:width(mt)],
                                        ALU.mult).then_inc(r_decayed, 1)

            def grouped(ap):
                return ap.rearrange("p (g e) -> p g e", e=HD)

            def spread(ap):
                return ap.unsqueeze(2).to_broadcast([P, HEADS, HD])

            def ret_center(k):
                dve.wait_ge(r_rows, k + 1)
                nc.vector.tensor_reduce(gsum[:], grouped(bank[YR_BANK][:]), AX.X, ALU.add).then_inc(r_sum, 1)
                dve.wait_ge(r_sum, k + 1)
                nc.vector.tensor_scalar(gneg[:], gsum[:], -1.0 / HD, None, ALU.mult).then_inc(r_neg, 1)
                dve.wait_ge(r_neg, k + 1)
                nc.vector.tensor_tensor(grouped(centered), grouped(bank[YR_BANK][:]), spread(gneg[:]),
                                        ALU.add).then_inc(r_centered, 1)

            def ret_variance(k):
                dve.wait_ge(r_sq, k + 1)
                nc.vector.tensor_reduce(gvar[:], grouped(squares), AX.X, ALU.add).then_inc(r_var, 1)

            def ret_norm(k):
                dve.wait_ge(r_rstd, k + 1)
                nc.vector.tensor_tensor(grouped(centered), grouped(centered), spread(grstd[:]),
                                        ALU.mult).then_inc(r_normed, 1)

            def ret_gate(k):
                dve.wait_ge(r_turned, k + 1)
                nc.vector.tensor_tensor(gated, bank[YR_BANK][:], gate, ALU.mult).then_inc(r_gated, 1)

            def y_slice(half, k):
                return (yT[:, half, k, :] if isinstance(k, int)
                        else yT[:, half, bass.ds(k, 1), :].rearrange("p o c -> p (o c)"))

            def ret_low(k):
                dve.wait_ge(r_yhi, k + 1)
                nc.vector.tensor_tensor(y_slice(1, k + PAIRS), gated, f32(y_slice(0, k + PAIRS)),
                                        ALU.subtract).then_inc(r_ylo, 1)

            def bias_and_max(i, u, first):
                h, w = u // 4, width(u % 4)
                if u == 0:
                    dve.wait_ge(btab_loaded, 16 * i + 16)
                dve.wait_ge(a_scores, 8 * i + u + 1)
                if u >= 3:
                    dve.wait_ge(a_turned, 8 * i + u - 2)
                if not first:
                    dve.sem_inc(bias_granted, 1)
                nc.vector.tensor_tensor_reduce(out=probs[:, u % 3, 0:w], in0=bank[S_BANK[u % 2]][:, 0:w],
                                               in1=btab[:, h, 0:w], scale=-0.125, scalar=3.0e38, op0=ALU.add,
                                               op1=ALU.min, accum_out=negmax[:, u:u + 1]).then_inc(a_biased, 1)

            def normalise(i, u):
                w = width(u % 4)
                dve.wait_ge(a_exp, 8 * i + u + 1)
                nc.vector.reciprocal(rowinv[:, u:u + 1], rowsum[:, u:u + 1]).then_inc(a_inv, 1)
                dve.wait_ge(a_inv, 8 * i + u + 1)
                nc.vector.tensor_scalar(probs[:, u % 3, 0:w], probs[:, u % 3, 0:w], rowinv[:, u:u + 1], None,
                                        ALU.mult).then_inc(a_probs, 1)

            def rotate(i, j, first):
                side = j - KR
                dve.wait_ge(swapped, 2 * i + side + 1)
                if side or not first:
                    dve.wait_ge(rq_lo, 2 * i + side)
                nc.vector.tensor_tensor(rotc, bank[UNIT_BANK[j]][:], rot[:, 0, :], ALU.mult).then_inc(cos_done, 1)
                nc.vector.tensor_tensor(rots, rots, rot[:, 1, :], ALU.mult).then_inc(sin_done, 1)

            def mixer_turn(i, first):
                for r in range(9):
                    if r == 0 and not first:
                        gate_finish(i - 1)
                    if r < 8 and not first:
                        ret_decay(i - 1, r)
                    if r == 3:
                        moba_stack(i, 0)
                    if r == 6:
                        moba_stack(i, 1)
                for u in range(12):
                    if 1 <= u < 9:
                        normalise(i, u - 1)
                    if u < 8:
                        bias_and_max(i, u, first)
                    if not first:
                        if u == 2:
                            ret_center(i - 1)
                        if u == 4:
                            ret_variance(i - 1)
                        if u == 5:
                            ret_norm(i - 1)
                        if u == 7:
                            ret_gate(i - 1)
                        if u == 8:
                            ret_low(i - 1)
                    if u == 4:
                        rotate(i, KR, first)
                    if u == 6:
                        ret_stack(i, 0)
                    if u == 7:
                        rotate(i, QR, first)
                    if u == 9:
                        ret_stack(i, 1)
                dve.wait_ge(a_yhi, i + 1)
                nc.vector.tensor_tensor(y_slice(1, i), bank[YA_BANK][:], f32(y_slice(0, i)), ALU.subtract).then_inc(a_ylo, 1)

            mixer_turn(0, True)
            with dve.Fori(1, PAIRS) as i:
                mixer_turn(i, False)

            k = PAIRS - 1
            gate_finish(k)
            for r in range(8):
                ret_decay(k, r)
                if r in (1, 3, 5, 6):
                    split_lo(OUT0 + 2 + (1, 3, 5, 6).index(r))
            split_lo(OUT0 + 6)
            ret_center(k)
            ret_variance(k)
            split_lo(OUT0 + 7)
            ret_norm(k)
            split_lo(OUT0 + 8)
            ret_gate(k)
            ret_low(k)
            split_lo(OUT0 + 9)

            def out_gain(s):
                if s == 0:
                    dve.wait_ge(mix_post_gain_loaded, 16)
                if s >= 2:
                    dve.wait_ge(x_added, 2 * (s - 1))
                for half in range(2):
                    dve.wait_ge(o_sq, 2 * s + half + 1)
                    nc.vector.tensor_tensor(orow[:, s % 2, half * 512:half * 512 + 512], bank[O_BANK[s][half]][:],
                                            gains[:, 1, half * 512:half * 512 + 512], ALU.mult).then_inc(o_gained, 1)

            def out_residual(s):
                dve.wait_ge(o_rstd, s + 1)
                dve.wait_ge(o_gained, 2 * s + 2)
                for half in range(2):
                    cols = slice(half * 512, half * 512 + 512)
                    nc.vector.scalar_tensor_tensor(xs[:, s, cols], orow[:, s % 2, cols], rstd[:, 8 + s:9 + s],
                                                   xs[:, s, cols], ALU.mult, ALU.add).then_inc(x_added, 1)

            dve.wait_ge(norm2_gain_loaded, 16)
            for k in range(KT):
                split_lo(OUT0 + KT + k + 2)
                if k == 0:
                    out_gain(0)
                    out_residual(0)
                if k == 1:
                    out_gain(1)
                    out_residual(1)
                if k == 3:
                    normed_rows(ST)
                if k == 4:
                    normed_rows(ST + 1)
                if k == 5:
                    h_low(ST)
                if k == 7:
                    h_low(ST + 1)
            out_gain(2)
            out_residual(2)
            split_lo(UP0 + 2)
            out_gain(3)
            out_residual(3)
            normed_rows(ST + 2)
            split_lo(UP0 + 3)
            normed_rows(ST + 3)
            h_low(ST + 2)
            h_low(ST + 3)

            def up_post(i, j):
                t = 2 * i + ((FT if j % 2 else 0) + j // 2)
                c = (cb if j % 2 else ca)[:, j // 2, :]

                def col(tap):
                    a = 2 * FT * tap + t
                    return conv[:, a:a + 1] if isinstance(a, int) else conv[:, bass.ds(a, 1)]
                dve.wait_ge(tap2, 4 * i + (j + 1))
                nc.vector.scalar_tensor_tensor(c[:, 1:SEQ], bank[UP_BANK[j]][:, 0:SEQ - 1], col(1), c[:, 1:SEQ],
                                               ALU.mult, ALU.add).then_inc(tap1, 1)
                dve.wait_ge(tap1, 4 * i + (j + 1))
                nc.vector.scalar_tensor_tensor(c[:, 2:SEQ], bank[UP_BANK[j]][:, 0:SEQ - 2], col(0), c[:, 2:SEQ],
                                               ALU.mult, ALU.add).then_inc(tap0, 1)
                if j % 2:
                    pair = 2 * i + j // 2
                    dst = (fT[:, pair, :] if isinstance(pair, int)
                           else fT[:, bass.ds(pair, 1), :].rearrange("p o c -> p (o c)"))
                    dve.wait_ge(gelu_done, 2 * i + (j // 2 + 1))
                    dve.wait_ge(tap0, 4 * i + (j + 1))
                    nc.vector.tensor_tensor(dst, ca[:, j // 2, :], cb[:, j // 2, :], ALU.mult).then_inc(f_ready, 1)

            def down_gain(half, s):
                dve.wait_ge(down_rows, ST * half + s + 1)
                dve.wait_ge(o_sq, (2 + half) * ST + s + 1)
                nc.vector.tensor_tensor(finished(s, half), bank[DOWN_BANK[half][s]][:],
                                        gains[:, 1, half * 512:half * 512 + 512], ALU.mult).then_inc(down_gained, 1)

            def down_lo(n0, q, i):
                c = slot_of(n0 + q)
                dve.wait_ge(w_hi, 2 * i + (n0 + q + 1))
                nc.vector.tensor_tensor(ws[:, c, 1, :], raw[:, c, :], f32(ws[:, c, 0, :]), ALU.subtract).then_inc(w_lo, 1)
                for kk in range(2):
                    k = 4 * i + (2 * ((n0 - DOWN0) % SWEEP + q) + kk)
                    src = fT[:, k, :] if isinstance(k, int) else fT[:, bass.ds(k, 1), :].rearrange("p o c -> p (o c)")
                    dve.wait_ge(f_hi, 4 * i + (2 * (n0 - DOWN0 + q) + kk + 1))
                    nc.vector.tensor_tensor(yT[:, 1, 2 * c + kk, :], src, f32(yT[:, 0, 2 * c + kk, :]),
                                            ALU.subtract).then_inc(f_lo, 1)

            for j in range(4):
                if j >= 2:
                    split_lo(UP0 + 2 + j)
                up_post(0, j)
            with dve.Fori(1, SWEEP - 1) as i:
                for j in range(4):
                    split_lo(UP0 + 2 + j, i, 4)
                    up_post(i, j)
            for j in range(4):
                if j < 2:
                    split_lo(UP0 + 2 + j, SWEEP - 1, 4)
                else:
                    down_lo(DOWN0, j - 2, 0)
                up_post(SWEEP - 1, j)
            for sweep in range(2):
                first = DOWN0 + sweep * SWEEP
                if sweep:
                    for q in range(2):
                        down_lo(first, q, 0)
                    dve.wait_ge(ffn_post_gain_loaded, 16)
                    for s in range(ST):
                        down_gain(0, s)
                with dve.Fori(1, SWEEP // 2) as i:
                    for q in range(2):
                        down_lo(first, q, i)
                down_lo(first + SWEEP - 1, 0, 0)

            def down_residual(s):
                dve.wait_ge(o_rstd, ST + s + 1)
                dve.wait_ge(down_gained, ST + s + 1)
                for half in range(2):
                    nc.vector.scalar_tensor_tensor(finished(s, half), finished(s, half), rstd[:, 12 + s:13 + s],
                                                   xs[:, s, half * 512:half * 512 + 512],
                                                   ALU.mult, ALU.add).then_inc(down_added, 1)

            for s in range(ST):
                down_gain(1, s)
                down_residual(s)


def rotary_table():
    inv = np.float32(10000.0) ** (-np.arange(0, HD, 2, dtype=np.float32) / np.float32(HD))
    ang = (np.arange(SEQ, dtype=np.float32)[None, :] * inv.astype(np.float32)[:, None]).astype(np.float64)
    cos = np.tile(np.cos(ang), (4, 1))
    sin = np.concatenate([-np.sin(ang), np.sin(ang)] * 2, axis=0)
    return np.stack([cos, sin], axis=1).astype(np.float32)


def decay_vectors():
    gamma = 1.0 - 2.0 ** (-5.0 - np.arange(HEADS, dtype=np.float64))
    dist = np.arange(VEC) - (P - 1)
    return np.where(dist >= 0, gamma[:, None] ** np.maximum(dist, 0), 0.0).astype(np.float32) * np.float32(HD ** -0.5)


def bucket_onehot():
    dist = np.arange(VEC) - (P - 1)
    exact = BUCKETS // 2
    far = np.maximum(dist, 1).astype(np.float64)
    large = exact + np.floor(np.log(far / exact) / math.log(MAX_DIST / exact) * (BUCKETS - exact) + 1e-9).astype(np.int64)
    bucket = np.where(dist < exact, dist, np.minimum(large, BUCKETS - 1))
    bucket = np.where(dist < 0, BUCKETS, bucket)
    return (np.arange(BUCKETS + 1)[:, None] == bucket[None, :]).astype(np.float32)


_INS = ["x", "norm_mix_pre", "w_in", "rel_bias", "w_out", "norm_mix_post", "norm_ffn_pre", "w_up",
        "conv_w", "conv_b", "w_down", "norm_ffn_post"]


def kernel(**inputs):
    import numpy as _np
    import concourse.bacc as _bacc
    from concourse import mybir as _mybir
    from concourse.bass_utils import run_bass_kernel_spmd as _run

    nc = _bacc.Bacc("TRN2", target_bir_lowering=False, num_devices=1)
    arrays, args = {}, []
    given = [(name, _np.ascontiguousarray(inputs[name])) for name in _INS]
    given += [("rotary", rotary_table()), ("decay", decay_vectors()), ("onehot", bucket_onehot())]
    for name, a in given:
        arrays[f"in_{name}_dram"] = a
        args.append(nc.dram_tensor(f"in_{name}_dram", a.shape, _mybir.dt.from_np(a.dtype), kind="ExternalInput").ap())
    args.append(nc.dram_tensor("out_0_dram", (1, SEQ, D), _mybir.dt.float32, kind="ExternalOutput").ap())
    build(nc, *args)
    r = _run(nc, [arrays], core_ids=[0])
    return r.results[0]["out_0_dram"]
```
